# Optimizing a Trainium2 kernel written in Bass

```python
import jax, jax.numpy as jnp
from jax import lax
import numpy as np

D_MODEL = 1024
BATCH = 1
SEQ = 512
DEPTH = 1

GRID_W = 64
CTX_LEN = 256
D_MIX = D_MODEL
GLA_WIDTH = D_MIX // 2
POOL_WIDTH = D_MIX - GLA_WIDTH
GLA_HEADS = 4
GLA_DV = GLA_WIDTH // GLA_HEADS
GLA_DK = GLA_DV // 2
GLA_QK = GLA_HEADS * GLA_DK
GATE_RANK = 16
GATE_NORMALIZER = 16.0
GLA_CHUNK = 64
POOL_GROUPS = 4
POOL_GC = POOL_WIDTH // POOL_GROUPS
POOL_WINDOWS = (2, 4, 8, 16)
N_EXPERTS = 32
TOP_K = 4
D_FF = D_MODEL
SWIGLU_LIMIT = 7.0
SWIGLU_ALPHA = 1.702
EXPERT_BLOCK = 128
N_MOD = 6
EPS = 1e-6
D_IN = 2 * GLA_QK + 2 * GLA_WIDTH + 2 * GATE_RANK + POOL_WIDTH
SPLIT_POINTS = (GLA_QK, 2 * GLA_QK, 2 * GLA_QK + GLA_WIDTH, 2 * GLA_QK + 2 * GLA_WIDTH,
                2 * GLA_QK + 2 * GLA_WIDTH + GATE_RANK, 2 * GLA_QK + 2 * GLA_WIDTH + 2 * GATE_RANK)


def rmsnorm(x, w):
    xf = x.astype(jnp.float32)
    var = jnp.mean(xf * xf, axis=-1, keepdims=True)
    return (xf * lax.rsqrt(var + EPS) * w.astype(jnp.float32)).astype(x.dtype)

def modulate(h, shift, scale):
    return h * (1.0 + scale) + shift

def to_heads(t, d):
    b_, n, _ = t.shape
    return t.reshape(b_, n, GLA_HEADS, d).transpose(0, 2, 1, 3).astype(jnp.float32)

def mixer_inputs(p, w_gk_f, b_gk_f, w_gk_b, b_gk_b):
    q, k, v, g, r_f, r_b, pool_in = jnp.split(p, SPLIT_POINTS, axis=-1)
    gk_f = jax.nn.log_sigmoid((r_f @ w_gk_f + b_gk_f).astype(jnp.float32)) / GATE_NORMALIZER
    gk_b = jax.nn.log_sigmoid((r_b @ w_gk_b + b_gk_b).astype(jnp.float32)) / GATE_NORMALIZER
    return (to_heads(q, GLA_DK), to_heads(k, GLA_DK), to_heads(v, GLA_DV),
            to_heads(gk_f, GLA_DK), to_heads(gk_b, GLA_DK), g, pool_in)

def gla_chunked(q, k, v, gk, s0, with_output=True):
    b_, h_, t_, dk = q.shape
    dv = v.shape[-1]
    n_ch = t_ // GLA_CHUNK
    qc = q.reshape(b_, h_, n_ch, GLA_CHUNK, dk) * (dk ** -0.5)
    kc = k.reshape(b_, h_, n_ch, GLA_CHUNK, dk)
    vc = v.reshape(b_, h_, n_ch, GLA_CHUNK, dv)
    bcum = jnp.cumsum(gk.reshape(b_, h_, n_ch, GLA_CHUNK, dk), axis=3)
    b_last = bcum[:, :, :, -1:, :]
    u = jnp.einsum('bhnsk,bhnsv->bhnkv', kc * jnp.exp(b_last - bcum), vc)
    decay = jnp.exp(b_last[:, :, :, 0, :])

    def step(s, inp):
        d, un = inp
        return d[..., None] * s + un, s

    s_final, s_prev = lax.scan(step, s0, (jnp.moveaxis(decay, 2, 0), jnp.moveaxis(u, 2, 0)))
    if not with_output:
        return None, s_final
    s_prev = jnp.moveaxis(s_prev, 0, 2)
    b_mid = bcum[:, :, :, GLA_CHUNK // 2 - 1:GLA_CHUNK // 2, :]
    a = jnp.einsum('bhntk,bhnsk->bhnts', qc * jnp.exp(bcum - b_mid), kc * jnp.exp(b_mid - bcum))
    mask = jnp.tril(jnp.ones((GLA_CHUNK, GLA_CHUNK), dtype=bool))
    a = jnp.where(mask, a, 0.0)
    o = (jnp.einsum('bhnts,bhnsv->bhntv', a, vc)
         + jnp.einsum('bhntk,bhnkv->bhntv', qc * jnp.exp(bcum), s_prev))
    return o.reshape(b_, h_, t_, dv), s_final

def gla_bidir(q, k, v, gk_f, gk_b, s0_f, s0_b, with_output=True):
    flip = lambda t: jnp.flip(t, axis=2)
    o_f, s_f = gla_chunked(q, k, v, gk_f, s0_f, with_output)
    o_b, s_b = gla_chunked(flip(q), flip(k), flip(v), flip(gk_b), s0_b, with_output)
    o = o_f + flip(o_b) if with_output else None
    return o, s_f, s_b

def gla_output(o, g, w_norm):
    b_, _, n, _ = o.shape
    o = o.transpose(0, 2, 1, 3)
    o = o * lax.rsqrt(jnp.mean(o * o, axis=-1, keepdims=True) + EPS) * w_norm.astype(jnp.float32)
    gate = jax.nn.silu(g.astype(jnp.float32)).reshape(o.shape)
    return (o * gate).reshape(b_, n, GLA_WIDTH)

def window_bounds(pos, w, length):
    lo = w // 2
    hi = w - 1 - lo
    return jnp.clip(pos - lo, 0, length), jnp.clip(pos + hi + 1, 0, length)

def pool_grid(xp, rows):
    b_, n, _ = xp.shape
    xf = xp.astype(jnp.float32).reshape(b_, rows, GRID_W, POOL_GROUPS, POOL_GC)
    sat = jnp.pad(jnp.cumsum(jnp.cumsum(xf, axis=1), axis=2), ((0, 0), (1, 0), (1, 0), (0, 0), (0, 0)))
    r = jnp.arange(rows)
    col = jnp.arange(GRID_W)
    outs = []
    for gi, w in enumerate(POOL_WINDOWS):
        r0, r1 = window_bounds(r, w, rows)
        c0, c1 = window_bounds(col, w, GRID_W)
        s = sat[:, :, :, gi]
        s_r1, s_r0 = s[:, r1], s[:, r0]
        tot = s_r1[:, :, c1] - s_r0[:, :, c1] - s_r1[:, :, c0] + s_r0[:, :, c0]
        cnt = ((r1 - r0)[:, None] * (c1 - c0)[None, :]).astype(jnp.float32)
        outs.append(tot / cnt[None, :, :, None])
    mean = jnp.stack(outs, axis=3)
    return (mean - xf).reshape(b_, n, POOL_GROUPS, POOL_GC)

def pool_seq(xp):
    b_, n, _ = xp.shape
    xf = xp.astype(jnp.float32).reshape(b_, n, POOL_GROUPS, POOL_GC)
    cs = jnp.pad(jnp.cumsum(xf, axis=1), ((0, 0), (1, 0), (0, 0), (0, 0)))
    pos = jnp.arange(n)
    outs = []
    for gi, w in enumerate(POOL_WINDOWS):
        i0, i1 = window_bounds(pos, w, n)
        outs.append((cs[:, i1, gi] - cs[:, i0, gi]) / (i1 - i0).astype(jnp.float32)[None, :, None])
    return jnp.stack(outs, axis=2) - xf

def pool_project(pooled, w_pool, pool_scale):
    b_, n = pooled.shape[:2]
    y = jnp.einsum('bngc,gcd->bngd', pooled, w_pool.astype(jnp.float32)).reshape(b_, n, POOL_WIDTH)
    return y * pool_scale.astype(jnp.float32)

def moe(h, w_router, b_router, w_gu, b_gu, w_down, b_down):
    shp = h.shape
    xt = h.reshape(-1, D_MODEL)
    n_tok = xt.shape[0]
    n_assign = n_tok * TOP_K
    logits = (xt @ w_router + b_router).astype(jnp.float32)
    top_vals, top_idx = lax.top_k(logits, TOP_K)
    weights = jax.nn.softmax(top_vals, axis=-1)
    flat_e = top_idx.reshape(-1)
    flat_tok = jnp.repeat(jnp.arange(n_tok, dtype=jnp.int32), TOP_K)
    flat_w = weights.reshape(-1)
    order = jnp.argsort(flat_e)
    sorted_e = flat_e[order]
    counts = jnp.bincount(flat_e, length=N_EXPERTS)
    padded = (counts + EXPERT_BLOCK - 1) // EXPERT_BLOCK * EXPERT_BLOCK
    start_unpad = jnp.cumsum(counts) - counts
    pad_end = jnp.cumsum(padded)
    start_pad = pad_end - padded
    dest = start_pad[sorted_e] + (jnp.arange(n_assign) - start_unpad[sorted_e])
    n_pad = n_assign + N_EXPERTS * EXPERT_BLOCK
    n_blocks = n_pad // EXPERT_BLOCK
    buf_tok = jnp.full((n_pad,), n_tok, dtype=jnp.int32).at[dest].set(flat_tok[order])
    buf_w = jnp.zeros((n_pad,), jnp.float32).at[dest].set(flat_w[order])
    block_e = jnp.minimum(jnp.searchsorted(pad_end, jnp.arange(n_blocks) * EXPERT_BLOCK, side='right'),
                          N_EXPERTS - 1)
    x_pad = jnp.concatenate([xt, jnp.zeros((1, D_MODEL), xt.dtype)], axis=0)
    xb = x_pad[buf_tok].reshape(n_blocks, EXPERT_BLOCK, D_MODEL)

    def expert_block(args):
        xblk, e = args
        gu = xblk @ w_gu[e] + b_gu[e]
        gate, up = jnp.split(gu, 2, axis=-1)
        gate = jnp.minimum(gate, SWIGLU_LIMIT)
        up = jnp.clip(up, -SWIGLU_LIMIT, SWIGLU_LIMIT)
        act = (up + 1.0) * gate * jax.nn.sigmoid(SWIGLU_ALPHA * gate)
        return act @ w_down[e] + b_down[e]

    yb = lax.map(expert_block, (xb, block_e)).reshape(n_pad, D_MODEL)
    y = jnp.zeros((n_tok + 1, D_MODEL), yb.dtype).at[buf_tok].add(yb * buf_w[:, None].astype(yb.dtype))
    return y[:n_tok].reshape(shp)

def first_inputs(seed: int = 0) -> dict:
    key = jax.random.key(seed)
    ks = jax.random.split(key, 32)
    nrm = lambda k, shp, s: jax.random.normal(k, shp, jnp.float32) * s
    L, D, E = DEPTH, D_MODEL, N_EXPERTS
    return {
        "x": nrm(ks[0], (BATCH, SEQ, D), 1.0),
        "c": nrm(ks[1], (BATCH, D), 1.0),
        "ctx": nrm(ks[2], (BATCH, CTX_LEN, D), 1.0),
        "c_ctx": nrm(ks[3], (D,), 1.0),
        "w_ada": nrm(ks[4], (L, D, N_MOD * D), 0.5 * D ** -0.5),
        "b_ada": nrm(ks[5], (L, N_MOD * D), 0.02),
        "norm_mix_w": 1.0 + nrm(ks[6], (L, D), 0.02),
        "norm_mlp_w": 1.0 + nrm(ks[7], (L, D), 0.02),
        "w_in": nrm(ks[8], (L, D, D_IN), D ** -0.5),
        "w_gk_f": nrm(ks[9], (L, GATE_RANK, GLA_QK), GATE_RANK ** -0.5),
        "b_gk_f": jax.random.uniform(ks[10], (L, GLA_QK), jnp.float32, -2.0, 4.0),
        "w_gk_b": nrm(ks[11], (L, GATE_RANK, GLA_QK), GATE_RANK ** -0.5),
        "b_gk_b": jax.random.uniform(ks[12], (L, GLA_QK), jnp.float32, -2.0, 4.0),
        "gla_norm_w": 1.0 + nrm(ks[13], (L, GLA_DV), 0.02),
        "w_pool": nrm(ks[14], (L, POOL_GROUPS, POOL_GC, POOL_GC), POOL_GC ** -0.5),
        "pool_scale": 1.0 + nrm(ks[15], (L, POOL_WIDTH), 0.1),
        "w_out": nrm(ks[16], (L, D_MIX, D), D_MIX ** -0.5),
        "w_router": nrm(ks[17], (L, D, E), D ** -0.5),
        "b_router": nrm(ks[18], (L, E), 0.01),
        "w_gu": nrm(ks[19], (L, E, D, 2 * D_FF), D ** -0.5),
        "b_gu": nrm(ks[20], (L, E, 2 * D_FF), 0.02),
        "w_down": nrm(ks[21], (L, E, D_FF, D), D_FF ** -0.5),
        "b_down": nrm(ks[22], (L, E, D), 0.02),
        "final_norm_w": 1.0 + nrm(ks[23], (D,), 0.02),
    }

def first_block(x, c, ctx, c_ctx, w_ada, b_ada, norm_mix_w, norm_mlp_w, w_in, w_gk_f, b_gk_f, w_gk_b,
              b_gk_b, gla_norm_w, w_pool, pool_scale, w_out, w_router, b_router, w_gu, b_gu, w_down,
              b_down, final_norm_w):
    h, hc = x, ctx
    b_, n_lat, _ = x.shape
    rows = n_lat // GRID_W
    for l in range(DEPTH):
        last = l == DEPTH - 1
        mod_x = (jax.nn.silu(c) @ w_ada[l] + b_ada[l])[:, None, :]
        mod_c = jax.nn.silu(c_ctx) @ w_ada[l] + b_ada[l]
        sh1, sc1, g1, sh2, sc2, g2 = jnp.split(mod_x, N_MOD, axis=-1)
        csh1, csc1, cg1, csh2, csc2, cg2 = jnp.split(mod_c, N_MOD, axis=-1)

        p_x = modulate(rmsnorm(h, norm_mix_w[l]), sh1, sc1) @ w_in[l]
        p_c = modulate(rmsnorm(hc, norm_mix_w[l]), csh1, csc1) @ w_in[l]
        qx, kx, vx, gkfx, gkbx, gx, poolx = mixer_inputs(p_x, w_gk_f[l], b_gk_f[l], w_gk_b[l], b_gk_b[l])
        qc, kc, vc, gkfc, gkbc, gc, poolc = mixer_inputs(p_c, w_gk_f[l], b_gk_f[l], w_gk_b[l], b_gk_b[l])

        s0 = jnp.zeros((b_, GLA_HEADS, GLA_DK, GLA_DV), jnp.float32)
        o_c, s_f, s_b = gla_bidir(qc, kc, vc, gkfc, gkbc, s0, s0, with_output=not last)
        o_x, _, _ = gla_bidir(qx, kx, vx, gkfx, gkbx, s_f, s_b)

        mix_x = jnp.concatenate([gla_output(o_x, gx, gla_norm_w[l]),
                                 pool_project(pool_grid(poolx, rows), w_pool[l], pool_scale[l])], axis=-1)
        h = h + g1 * (mix_x.astype(h.dtype) @ w_out[l])

        if not last:
            mix_c = jnp.concatenate([gla_output(o_c, gc, gla_norm_w[l]),
                                     pool_project(pool_seq(poolc), w_pool[l], pool_scale[l])], axis=-1)
            hc = hc + cg1 * (mix_c.astype(hc.dtype) @ w_out[l])
            hc = hc + cg2 * moe(modulate(rmsnorm(hc, norm_mlp_w[l]), csh2, csc2),
                                w_router[l], b_router[l], w_gu[l], b_gu[l], w_down[l], b_down[l])

        h = h + g2 * moe(modulate(rmsnorm(h, norm_mlp_w[l]), sh2, sc2),
                         w_router[l], b_router[l], w_gu[l], b_gu[l], w_down[l], b_down[l])
    return rmsnorm(h, final_norm_w)


DEPTH_2 = 2

MIX_WIDTH = 2 * D_MODEL
FOURIER_WIDTH = MIX_WIDTH // 2
N_FOURIER_GROUPS = 4
FOURIER_GROUP = FOURIER_WIDTH // N_FOURIER_GROUPS
ATTN_WIDTH = MIX_WIDTH - FOURIER_WIDTH
HEAD_DIM = 128
N_Q_HEADS = ATTN_WIDTH // HEAD_DIM
N_KV_HEADS = 2
Q_PER_KV = N_Q_HEADS // N_KV_HEADS
KV_WIDTH = N_KV_HEADS * HEAD_DIM
Q_BLOCK = 128
ROPE_THETA = 10000.0
ROPE_AXIS_DIM = HEAD_DIM // 2
RNN_WIDTH = MIX_WIDTH
N_RNN_BLOCKS = 16
RNN_BLOCK = RNN_WIDTH // N_RNN_BLOCKS
CONV_WIDTH = 4
CONV_LEFT = 2
RG_LRU_C = 8.0
NORM_EPS = 1e-6
EVEN_IN_WIDTH = 2 * FOURIER_WIDTH + ATTN_WIDTH + 2 * KV_WIDTH + ATTN_WIDTH
EVEN_SPLITS = (FOURIER_WIDTH,
               2 * FOURIER_WIDTH,
               2 * FOURIER_WIDTH + ATTN_WIDTH,
               2 * FOURIER_WIDTH + ATTN_WIDTH + KV_WIDTH,
               2 * FOURIER_WIDTH + ATTN_WIDTH + 2 * KV_WIDTH)


def rms_norm(x, g):
    xf = x.astype(jnp.float32)
    y = xf * lax.rsqrt(jnp.mean(xf * xf, axis=-1, keepdims=True) + NORM_EPS)
    return (y * g.astype(jnp.float32)).astype(x.dtype)

def axial_rope_tables(seq_len):
    rows = seq_len // GRID_W
    row = jnp.broadcast_to(jnp.arange(rows)[:, None], (rows, GRID_W)).reshape(-1).astype(jnp.float32)
    col = jnp.broadcast_to(jnp.arange(GRID_W)[None, :], (rows, GRID_W)).reshape(-1).astype(jnp.float32)
    inv_freq = ROPE_THETA ** (-jnp.arange(0, ROPE_AXIS_DIM, 2, dtype=jnp.float32) / ROPE_AXIS_DIM)
    ang_r = row[:, None] * inv_freq[None, :]
    ang_c = col[:, None] * inv_freq[None, :]
    return (jnp.cos(ang_r), jnp.sin(ang_r), jnp.cos(ang_c), jnp.sin(ang_c))

def rope_half(x, cos, sin):
    x1, x2 = jnp.split(x, 2, axis=-1)
    c = cos[:, None, :]
    s = sin[:, None, :]
    return jnp.concatenate([x1 * c - x2 * s, x1 * s + x2 * c], axis=-1)

def axial_rope(x, tables):
    cos_r, sin_r, cos_c, sin_c = tables
    xf = x.astype(jnp.float32)
    x_row, x_col = jnp.split(xf, 2, axis=-1)
    out = jnp.concatenate([rope_half(x_row, cos_r, sin_r), rope_half(x_col, cos_c, sin_c)], axis=-1)
    return out.astype(x.dtype)

def blocked_attention(q, k, v):
    b, s = q.shape[0], q.shape[1]
    n_blocks = s // Q_BLOCK
    qb = q.reshape(b, n_blocks, Q_BLOCK, N_KV_HEADS, Q_PER_KV, HEAD_DIM).transpose(1, 0, 2, 3, 4, 5)
    scale = HEAD_DIM ** -0.5

    def one_block(q_blk):
        scores = jnp.einsum('bqhgd,bkhd->bhgqk', q_blk, k,
                            preferred_element_type=jnp.float32) * scale
        probs = jax.nn.softmax(scores, axis=-1).astype(v.dtype)
        return jnp.einsum('bhgqk,bkhd->bqhgd', probs, v)

    out = lax.map(one_block, qb)
    return out.transpose(1, 0, 2, 3, 4, 5).reshape(b, s, N_Q_HEADS * HEAD_DIM)

def fourier_attention_layer(x, norm_g, w_in, fourier_w, q_gain, k_gain, w_out, rope):
    b, s, _ = x.shape
    h = rms_norm(x, norm_g)
    proj = h @ w_in
    f_in, f_gate, q, k, v, a_gate = jnp.split(proj, EVEN_SPLITS, axis=-1)
    fg = f_in.astype(jnp.float32).reshape(b, s, N_FOURIER_GROUPS, FOURIER_GROUP)
    fmix = jnp.fft.fftn(fg, axes=(1, 3), norm="ortho").real.astype(x.dtype)
    fmix = jnp.einsum('bsgc,gce->bsge', fmix, fourier_w).reshape(b, s, FOURIER_WIDTH)
    f_out = fmix * jax.nn.silu(f_gate)
    q = rms_norm(q.reshape(b, s, N_Q_HEADS, HEAD_DIM), q_gain)
    k = rms_norm(k.reshape(b, s, N_KV_HEADS, HEAD_DIM), k_gain)
    v = v.reshape(b, s, N_KV_HEADS, HEAD_DIM)
    q = axial_rope(q, rope)
    k = axial_rope(k, rope)
    a_out = blocked_attention(q, k, v) * jax.nn.silu(a_gate)
    return x + jnp.concatenate([f_out, a_out], axis=-1) @ w_out

def rglru_scan(xc, w_a, b_a, w_x, b_x, lam, reverse):
    b, s, _ = xc.shape
    xb = xc.astype(jnp.float32).reshape(b, s, N_RNN_BLOCKS, RNN_BLOCK)
    r = jax.nn.sigmoid(jnp.einsum('bshc,hce->bshe', xb, w_a.astype(jnp.float32)) + b_a).reshape(b, s, RNN_WIDTH)
    i = jax.nn.sigmoid(jnp.einsum('bshc,hce->bshe', xb, w_x.astype(jnp.float32)) + b_x).reshape(b, s, RNN_WIDTH)
    log_a = -RG_LRU_C * r * jax.nn.softplus(-lam.astype(jnp.float32))
    a = jnp.exp(log_a)
    u = jnp.sqrt(-jnp.expm1(2.0 * log_a)) * (i * xb.reshape(b, s, RNN_WIDTH))

    def combine(left, right):
        a1, h1 = left
        a2, h2 = right
        return a1 * a2, a2 * h1 + h2

    _, hseq = lax.associative_scan(combine, (a, u), reverse=reverse, axis=1)
    return hseq

def rglru_layer(x, norm_g, w_in, conv_w, conv_b, w_a, b_a, w_x, b_x, lam, w_out):
    s = x.shape[1]
    h = rms_norm(x, norm_g)
    xr, gate = jnp.split(h @ w_in, 2, axis=-1)
    xp = jnp.pad(xr, ((0, 0), (CONV_LEFT, CONV_WIDTH - 1 - CONV_LEFT), (0, 0)))
    xc = conv_b + xp[:, 0:s] * conv_w[0]
    for j in range(1, CONV_WIDTH):
        xc = xc + xp[:, j:j + s] * conv_w[j]
    y = (rglru_scan(xc, w_a[0], b_a[0], w_x[0], b_x[0], lam[0], reverse=False)
         + rglru_scan(xc, w_a[1], b_a[1], w_x[1], b_x[1], lam[1], reverse=True))
    return x + (y.astype(x.dtype) * jax.nn.silu(gate)) @ w_out

def second_inputs(seed: int = 0) -> dict:
    key = jax.random.key(seed)
    ks = jax.random.split(key, 20)
    n_even = (DEPTH_2 + 1) // 2
    n_odd = DEPTH_2 // 2

    def nrm(k, shape, scale):
        return jax.random.normal(k, shape, jnp.float32) * scale

    x = nrm(ks[0], (BATCH, SEQ, D_MODEL), 1.0)
    even_norm = 1.0 + nrm(ks[1], (n_even, D_MODEL), 0.02)
    even_w_in = nrm(ks[2], (n_even, D_MODEL, EVEN_IN_WIDTH), D_MODEL ** -0.5)
    fourier_w = nrm(ks[3], (n_even, N_FOURIER_GROUPS, FOURIER_GROUP, FOURIER_GROUP), FOURIER_GROUP ** -0.5)
    q_gain = 1.0 + nrm(ks[4], (n_even, HEAD_DIM), 0.02)
    k_gain = 1.0 + nrm(ks[5], (n_even, HEAD_DIM), 0.02)
    even_w_out = nrm(ks[6], (n_even, MIX_WIDTH, D_MODEL), MIX_WIDTH ** -0.5)
    odd_norm = 1.0 + nrm(ks[7], (n_odd, D_MODEL), 0.02)
    odd_w_in = nrm(ks[8], (n_odd, D_MODEL, 2 * RNN_WIDTH), D_MODEL ** -0.5)
    conv_w = nrm(ks[9], (n_odd, CONV_WIDTH, RNN_WIDTH), CONV_WIDTH ** -0.5)
    conv_b = nrm(ks[10], (n_odd, RNN_WIDTH), 0.01)
    gate_a_w = nrm(ks[11], (n_odd, 2, N_RNN_BLOCKS, RNN_BLOCK, RNN_BLOCK), RNN_BLOCK ** -0.5)
    gate_a_b = nrm(ks[12], (n_odd, 2, N_RNN_BLOCKS, RNN_BLOCK), 0.01)
    gate_x_w = nrm(ks[13], (n_odd, 2, N_RNN_BLOCKS, RNN_BLOCK, RNN_BLOCK), RNN_BLOCK ** -0.5)
    gate_x_b = nrm(ks[14], (n_odd, 2, N_RNN_BLOCKS, RNN_BLOCK), 0.01)
    a_pow = jax.random.uniform(ks[15], (n_odd, 2, RNN_WIDTH), jnp.float32, minval=0.9, maxval=0.999)
    a0 = a_pow ** (1.0 / RG_LRU_C)
    rglru_lambda = jnp.log(a0) - jnp.log1p(-a0)
    odd_w_out = nrm(ks[16], (n_odd, RNN_WIDTH, D_MODEL), RNN_WIDTH ** -0.5)
    final_norm = 1.0 + nrm(ks[17], (D_MODEL,), 0.02)
    return {"x": x, "even_norm": even_norm, "even_w_in": even_w_in, "fourier_w": fourier_w,
            "q_gain": q_gain, "k_gain": k_gain, "even_w_out": even_w_out,
            "odd_norm": odd_norm, "odd_w_in": odd_w_in, "conv_w": conv_w, "conv_b": conv_b,
            "gate_a_w": gate_a_w, "gate_a_b": gate_a_b, "gate_x_w": gate_x_w, "gate_x_b": gate_x_b,
            "rglru_lambda": rglru_lambda, "odd_w_out": odd_w_out, "final_norm": final_norm}

def second_block(x, even_norm, even_w_in, fourier_w, q_gain, k_gain, even_w_out,
              odd_norm, odd_w_in, conv_w, conv_b, gate_a_w, gate_a_b, gate_x_w, gate_x_b,
              rglru_lambda, odd_w_out, final_norm):
    rope = axial_rope_tables(x.shape[1])
    h = x
    for layer in range(DEPTH_2):
        i = layer // 2
        if layer % 2 == 0:
            h = fourier_attention_layer(h, even_norm[i], even_w_in[i], fourier_w[i],
                                        q_gain[i], k_gain[i], even_w_out[i], rope)
        else:
            h = rglru_layer(h, odd_norm[i], odd_w_in[i], conv_w[i], conv_b[i],
                            gate_a_w[i], gate_a_b[i], gate_x_w[i], gate_x_b[i],
                            rglru_lambda[i], odd_w_out[i])
    return rms_norm(h, final_norm)


def setup_inputs(seed=0):
    out = dict(first_inputs(seed))
    for name, value in second_inputs(seed + 1).items():
        if name != "x":
            out[name + "_2"] = value
    return out


def reference(
    x, c, ctx, c_ctx, w_ada, b_ada, norm_mix_w, norm_mlp_w, w_in, w_gk_f, b_gk_f, w_gk_b,
    b_gk_b, gla_norm_w, w_pool, pool_scale, w_out, w_router, b_router, w_gu, b_gu, w_down,
    b_down, final_norm_w, even_norm_2, even_w_in_2, fourier_w_2, q_gain_2, k_gain_2,
    even_w_out_2, odd_norm_2, odd_w_in_2, conv_w_2, conv_b_2, gate_a_w_2, gate_a_b_2,
    gate_x_w_2, gate_x_b_2, rglru_lambda_2, odd_w_out_2, final_norm_2,
):
    x = first_block(
        x, c, ctx, c_ctx, w_ada, b_ada, norm_mix_w, norm_mlp_w, w_in, w_gk_f, b_gk_f, w_gk_b,
        b_gk_b, gla_norm_w, w_pool, pool_scale, w_out, w_router, b_router, w_gu, b_gu, w_down,
        b_down, final_norm_w,
    )
    return second_block(
        x, even_norm_2, even_w_in_2, fourier_w_2, q_gain_2, k_gain_2, even_w_out_2, odd_norm_2,
        odd_w_in_2, conv_w_2, conv_b_2, gate_a_w_2, gate_a_b_2, gate_x_w_2, gate_x_b_2,
        rglru_lambda_2, odd_w_out_2, final_norm_2,
    )


_drawn_inputs = setup_inputs


def setup_inputs(seed=0):
    import zlib

    import numpy as np

    out = dict(_drawn_inputs(seed))
    spreads = {}
    factors = {'norm_mix_w': 4.42,
     'norm_mlp_w': 2.998,
     'gla_norm_w': 7.949,
     'b_router': 4.036,
     'b_gu': 8.0,
     'b_down': 8.0,
     'even_norm_2': 6.114,
     'q_gain_2': 8.0,
     'k_gain_2': 8.0,
     'odd_norm_2': 13.984,
     'gate_a_b_2': 64.0,
     'gate_x_b_2': 62.292,
     'final_norm_2': 7.999,
     'conv_b_2': 6.208}
    for name, (base, spread) in spreads.items():
        noise = np.random.default_rng([zlib.crc32(name.encode()), seed]).standard_normal(out[name].shape)
        drawn = base * np.exp(spread * noise) if base else spread * noise
        out[name] = __import__('jax').numpy.asarray(drawn.astype(out[name].dtype))
    for name, factor in factors.items():
        out[name] = (out[name] * factor).astype(out[name].dtype)
    return out
```

```python
from collections import namedtuple
from contextlib import ExitStack

import concourse.bass as bass
from concourse import mybir

F32 = mybir.dt.float32
BF16 = mybir.dt.bfloat16
U32 = mybir.dt.uint32
ALU = mybir.AluOpType
ACT = mybir.ActivationFunctionType
AX = mybir.AxisListType

P = 128
D = 1024
KD = D // P
T = 512
NT = T // P
TC = 256
NTC = TC // P
BANK = 512
H, DK, DV, CHUNK = 4, 64, 128, 64
NCH, NCHC = T // CHUNK, TC // CHUNK
E, TOPK, FF = 32, 4, 1024
CAP = 128
XB = T * TOPK // (CAP + 1)
EPS = 1e-6
SLOTS, SLOT = 12, 2048
MIX_SLOTS = 8
LATE_SLOTS = 8
HD, NQ, NKV = 128, 8, 2
RNN = 2048
NR = RNN // P

C_ID, C_MF, C_MB, C_IOTA1, C_TRI, C_ONES = 0, 128, 256, 384, 512, 640
C_IOTA32, C_TOK, C_RESET, C_XI, C_ID3, C_N = 768, 800, 804, 1572, 1588, 1624

VECS = [("c", KD), ("c_ctx", KD), ("norm_mix_w", KD), ("b_ada", 6 * KD), ("norm_mlp_w", KD), ("b_gk_f", 2),
        ("b_gk_b", 2), ("gla_norm_w", 1), ("pool_scale", 4), ("even_norm_2", KD), ("odd_norm_2", KD),
        ("conv_b_2", NR),
        ("conv_w_2", 4 * NR), ("gate_a_b_2", 2 * NR), ("gate_x_b_2", 2 * NR), ("rglru_lambda_2", 2 * NR)]


def vec_places():
    at, out = 0, {}
    for name, n in VECS:
        if at // P != (at + n - 1) // P:
            at = (at // P + 1) * P
        out[name] = at
        at += n
    assert at <= 3 * P
    return out


VEC = vec_places()


class Signal:

    def __init__(self, sem):
        self.sem, self.n = sem, 0

    def on(self, instruction, by=1):
        instruction.then_inc(self.sem, by)
        self.n += by
        return self.n

    def wait(self, engine):
        engine.wait_ge(self.sem, self.n)


class Job:

    def __init__(self, pipe, index, bank, engine, emptied, before):
        self.pipe, self.index, self.bank, self.engine, self.emptied, self.before = \
            pipe, index, bank, engine, emptied, before

    def open(self, pe):
        if self.before is not None:
            pe.wait_ge(self.pipe.free[self.before.engine], self.before.emptied)

    def done(self, matmul):
        matmul.then_inc(self.pipe.filled, 1)

    def filled(self, eng):
        eng.wait_ge(self.pipe.filled, self.index)

    def empty(self, instruction):
        instruction.then_inc(self.pipe.free[self.engine], 1)

    def emptied_for(self, eng):
        eng.wait_ge(self.pipe.free[self.engine], self.emptied)


class Psum:

    def __init__(self, filled, free_act, free_dve):
        self.filled, self.free = filled, {"act": free_act, "dve": free_dve}
        self.n, self.count, self.last = 0, {"act": 0, "dve": 0}, {}

    def job(self, bank, engine):
        self.n += 1
        self.count[engine] += 1
        j = Job(self, self.n, bank, engine, self.count[engine], self.last.get(bank))
        self.last[bank] = j
        return j


class Stream:

    def __init__(self, ring, ready, used):
        self.ring, self.ready, self.used = ring, ready, used
        self.tiles, self.loaded, self.taken, self.owed = [], 0, 0, 0
        self.width, self.first, self.held, self.landed = SLOTS, 0, {}, [0] * SLOTS

    def turn(self, width):
        self.width, self.first = width, len(self.tiles)

    def add(self, pieces, shape):
        n = len(self.tiles)
        slot = (n - self.first) % self.width
        count = 1
        for x in shape:
            count *= x
        flat = self.ring[:, slot, 0:count]
        view = flat.rearrange("p (k n) -> p k n", k=shape[0]) if len(shape) == 2 else flat
        dmas = pieces(view)
        self.landed[slot] += 16 * len(dmas)
        self.tiles.append((slot, view, dmas, self.landed[slot], self.held.get(slot, -1), shape))
        self.held[slot] = n

    def load(self, sp, end, slots=SLOTS):
        while self.loaded < len(self.tiles):
            slot, _, dmas, _, before, _ = self.tiles[self.loaded]
            if slot >= slots or before > end - 2:
                return
            if before >= 0:
                sp.wait_ge(self.used, before + 1)
            for dst, src in dmas:
                sp.dma_start(dst, src).then_inc(self.ready[slot], 16)
            self.loaded += 1

    def take(self, pe):
        slot, view, _, landed, _, _ = self.tiles[self.taken]
        pe.wait_ge(self.ready[slot], landed)
        self.taken += 1
        return view

    def release(self, matmul):
        matmul.then_inc(self.used, 1 + self.owed)
        self.owed = 0

    def owe(self):
        self.owed += 1

    def settle(self, matmul):
        if self.owed:
            matmul.then_inc(self.used, self.owed)
            self.owed = 0


EXPERT_SIGNALS = ("onehot_ready", "ids_done", "ids_read", "gathered", "xT_done", "xeT_read", "sel_ready", "gate_done",
                  "up_done", "gu_read", "sig_ready", "ug_ready", "act_ready", "aT_done", "aT_read", "y_done", "y_read",
                  "y_stored", "marked")
Expert = namedtuple("Expert", EXPERT_SIGNALS)
NORM_SIGNALS = ("sum", "mean", "root", "inverse", "scaled")
Norm = namedtuple("Norm", NORM_SIGNALS)


def build(nc, A, out):
    ctx = ExitStack()
    with ctx:
        def sbuf(name, shape, dt=F32, scope=ctx):
            return scope.enter_context(nc.sbuf_tensor(name, shape, dt))

        def sem(name):
            return ctx.enter_context(nc.semaphore(name))

        def signal(name):
            return Signal(sem(name))

        ps = ctx.enter_context(nc.psum_tensor("ps", [P, 8, BANK], F32))
        ring = sbuf("ring", [P, SLOTS, SLOT])
        cst = sbuf("cst", [P, C_N])
        vec = sbuf("vec", [P, 3 * P])
        res = sbuf("res", [P, NT, D])
        stat = sbuf("stat", [P, 64])

        stream = Stream(ring, [sem(f"slot_ready{i}") for i in range(SLOTS)], sem("slot_used"))
        psum = Psum(sem("psum_filled"), sem("psum_free_act"), sem("psum_free_dve"))
        dve_step = signal("dve_step")
        stored = signal("stored")

        ident = cst[:, C_ID:C_ID + P]
        ones = cst[:, C_ONES:C_ONES + P]

        def vcol(name, i=0, n=1):
            return vec[:, VEC[name] + i:VEC[name] + i + n]

        xn_dram = nc.dram_tensor("xn_scratch", (T, D), F32, kind="Internal").ap()
        y_dram = nc.dram_tensor("y_scratch", ((E + XB) * CAP, D), F32, kind="Internal").ap()
        row_blocks = y_dram.rearrange("(b s) n -> b s n", s=CAP)

        def ktiles(w, k0, ks, c0, c1):
            return w[k0 * P:(k0 + ks) * P, c0:c1].rearrange("(k p) n -> p k n", p=P)

        def add(src, *shape):
            stream.add(lambda view: [(view, src)], shape)

        def add_panel(w, k_all, per, c0, c1):
            for k0 in range(0, k_all, per):
                ks = min(per, k_all - k0)
                add(ktiles(w, k0, ks, c0, c1), ks, c1 - c0)

        def rows(w):
            return w.rearrange("(k p) n -> p k n", p=P)

        w_ada, w_in = A["w_ada"][0], A["w_in"][0]
        stream.turn(MIX_SLOTS)
        add_panel(w_ada, KD, 1, 0, 2 * D)
        add_panel(w_in, KD, 2, 0, 1024)
        add_panel(w_in, KD, 3, 1024, 1568)
        add_panel(w_in, KD, 4, 1568, 2080)
        end_inputs = len(stream.tiles)
        add_panel(w_ada, KD, 2, 2 * D, 3 * D)
        add_panel(w_ada, KD, 1, 3 * D, 5 * D)
        add_panel(w_ada, KD, 2, 5 * D, 6 * D)
        for g in range(4):
            add(rows(A["pool_mat"][g]), NT, T)
        add(A["w_pool"][0].rearrange("g p n -> p g n"), 4, P)
        end_gates = len(stream.tiles)
        add_panel(A["w_out"][0], KD, 2, 0, D)
        add(rows(A["w_router"][0]), KD, E)
        end_mix = len(stream.tiles)
        w_gu, w_down = A["w_gu"][0], A["w_down"][0]

        def add_moe(e, js):
            for j in js:
                if j < 8:
                    add(w_gu[e, j * P:(j + 1) * P, :], 2 * FF)
                else:
                    add(ktiles(w_down[e], 2 * (j - 8), 2, 0, D), 2, D)

        stream.turn(SLOTS)
        moe0 = len(stream.tiles)
        add_moe(0, range(8))
        for e in range(1, E):
            add_moe(e, range(8))
            add_moe(e - 1, range(8, 12))
        add_moe(E - 1, range(8, 12))
        end_moe = len(stream.tiles)
        stream.turn(LATE_SLOTS)
        w_even = A["even_w_in_2"][0]
        add_panel(w_even, KD, 2, D, 2 * D)
        add_panel(w_even, KD, 2, 0, D)
        add(rows(A["dft_c"]), 2, 512)
        add(rows(A["dft_s"][0]), NT, T)
        add(rows(A["dft_s"][1]), NT, T)
        add(A["fourier_w_2"][0].rearrange("g (k p) n -> p (g k) n", p=P), 8, 256)
        end_fourier = len(stream.tiles)
        add_panel(w_even, KD, 4, 3 * D, 3 * D + 512)
        add_panel(w_even, KD, 2, 2 * D, 3 * D)
        add_panel(w_even, KD, 2, 3 * D + 512, 4 * D + 512)
        end_qkv = len(stream.tiles)
        add_panel(A["even_w_out_2"][0], 2 * KD, 2, 0, D)
        end_even = len(stream.tiles)
        w_odd = A["odd_w_in_2"][0]

        def odd_pieces(p, k0):
            def pieces(view):
                return [(view[:, k, :].rearrange("p (s n) -> p s n", s=2),
                         w_odd[(k0 + k) * P:(k0 + k + 1) * P, :].rearrange("p (s n) -> p s n", s=2)
                         [:, :, p * 512:(p + 1) * 512]) for k in range(2)]
            return pieces

        def gate_pieces(p):
            def pieces(view):
                return [(view[:, (2 * d + g) * 4:(2 * d + g) * 4 + 4, :],
                         w[d, 4 * p:4 * p + 4].rearrange("b p n -> p b n"))
                        for d in range(2) for g, w in enumerate((A["gate_a_w_2"][0], A["gate_x_w_2"][0]))]
            return pieces

        for p in range(4):
            for k0 in range(0, KD, 2):
                stream.add(odd_pieces(p, k0), (2, 1024))
            stream.add(gate_pieces(p), (16, P))
        end_odd_in = len(stream.tiles)
        add_panel(A["odd_w_out_2"][0], 2 * KD, 2, 0, D)
        take = stream.take

        def bank(b, n=BANK, rows=P):
            return ps[0:rows, b, 0:n]

        def project(pe, n_tiles, jobs, release=True, before=None):
            k = 0
            for i in range(n_tiles):
                w = take(pe)
                ks = stream.tiles[stream.taken - 1][5][0]
                for kk in range(ks):
                    first, last = k == 0, i == n_tiles - 1 and kk == ks - 1
                    if before and k in before:
                        before[k]()
                    for job, dst, left, right in jobs:
                        if first:
                            job.open(pe)
                        mm = nc.tensor.matmul(dst, left(k, w, kk), right(k, w, kk), start=first, stop=last)
                        if first:
                            stream.settle(mm)
                        if last:
                            job.done(mm)
                    k += 1
                if release:
                    if i == n_tiles - 1:
                        stream.owe()
                    else:
                        stream.release(mm)

        def vector_rows(pe, jobs):
            project(pe, KD, [(j, bank(j.bank, BANK, 2), lambda k, w, kk: scol[:, k, :],
                              lambda k, w, kk, i=i: w[:, kk, i * BANK:(i + 1) * BANK]) for i, j in enumerate(jobs)])

        def turn_vector_rows(pe, jobs, j, rows):
            jobs[-1].emptied_for(pe)
            j.open(pe)
            for f in range(2 * KD):
                mm = nc.tensor.transpose(ps[:, j.bank, 2 * f:2 * f + 2], rows[:, f * P:(f + 1) * P], ident[0:2, 0:2])
            j.done(mm)

        g2b = sbuf("g2b", [P, D])
        mod2 = sbuf("mod2", [P, 2 * KD, 2])
        posm = sbuf("posm", [P, NT, E + 3])
        posx = sbuf("posx", [P, NT, XB])
        wk = sbuf("wk", [P, NT, TOPK])
        wtok = sbuf("wtok", [P, NT, E])
        dest = sbuf("dest", [P, NT * TOPK], U32)
        xlist = sbuf("xlist", [P, XB + 1], U32)
        xends = sbuf("xends", [P, 2, E])
        mix_scope = ctx.enter_context(ExitStack())
        sgT = sbuf("sgT", [P, H, T], scope=mix_scope)
        qT = sbuf("qT", [P, 2, T], scope=mix_scope)
        kT = sbuf("kT", [P, 2, T + TC], scope=mix_scope)
        rT = sbuf("rT", [32, T + TC], scope=mix_scope)
        vtok = sbuf("vtok", [P, NT + NTC, H * DV], scope=mix_scope)
        ptok = sbuf("ptok", [P, NT, 512], scope=mix_scope)
        scol = sbuf("scol", [P, KD, 2], scope=mix_scope)
        wgk = sbuf("wgk", [32, 2, 256], scope=mix_scope)
        wgk_loads = signal("wgk_loads")
        in_scope = ctx.enter_context(ExitStack())
        xc = sbuf("xc", [P, NTC, D], scope=in_scope)
        junk = ptok[:, 0:2, :].rearrange("p t n -> p (t n)")
        hT = sbuf("hT", [P, KD, T + TC], scope=in_scope)
        vrow = sbuf("vrow", [P, 3, P], scope=in_scope)
        mod1 = sbuf("mod1", [P, 2 * KD, 2], scope=in_scope)
        amix = sbuf("amix", [P, KD, 2], scope=in_scope)

        def xtile(t):
            return res[:, t, :] if t < NT else xc[:, t - NT, :]

        zeroed = signal("zeroed")
        rms_sum = signal("rms_sum")
        rms_mean = signal("rms_mean")
        rms_root = signal("rms_root")
        xn_ready = signal("xn_ready")
        scol_ready = signal("scol_ready")
        mod_ready = signal("mod_ready")

        j_vec = [psum.job(0, "dve")]
        j_rows = [psum.job(4 + i, "dve") for i in range(4)]
        j_mod = [psum.job(1, "dve")]
        mod_rows = ptok[0:2, :, :].rearrange("p t n -> p (t n)")
        vec_loads = signal("vec_loads")
        rows_loads = signal("rows_loads")
        j_tr = []
        for k in range(KD):
            j_tr.append((psum.job(2 + k % 3, "act"), psum.job(5 + k % 3, "dve")))
        j_qk = [psum.job(b, "act") for b in range(4)]
        j_v = [psum.job(4 + t, "dve") for t in range(NT)]
        j_kc = [psum.job(0, "act"), psum.job(1, "act")]
        j_vc = [psum.job(2 + t, "dve") for t in range(NTC)]
        j_g = [psum.job(4 + b, "act") for b in range(4)]
        j_r = psum.job(0, "dve")
        j_rc = psum.job(1, "dve")
        j_pool = [psum.job(2 + t, "dve") for t in range(NT)]

        def load_vectors(eng, which):
            for name, n in VECS[which::2]:
                at = VEC[name]
                vec_loads.on(eng.dma_start(vrow[at % P:at % P + n, at // P, :], A[name]), 16)

        with nc.Block() as block:
            @block.sync
            def _(sp):
                vec_loads.on(sp.dma_start(cst[:], A["cst"]), 16)
                sp.wait_ge(zeroed.sem, 2)
                load_vectors(sp, 1)
                stream.load(sp, end_inputs, MIX_SLOTS)

            @block.gpsimd
            def _(pool):
                zeroed.on(nc.gpsimd.memset(vrow[:], 0.0))
                zeroed.on(nc.gpsimd.memset(wgk[:], 0.0))
                rows_loads.on(pool.dma_start(res[:], A["x"][0].rearrange("(t p) n -> p t n", p=P)), 16)
                rows_loads.on(pool.dma_start(xc[:], A["ctx"][0].rearrange("(t p) n -> p t n", p=P)), 16)

            @block.scalar
            def _(act):
                act.wait_ge(zeroed.sem, 2)
                load_vectors(act, 0)
                wgk_loads.on(act.dma_start(wgk[0:16, 0, :], A["w_gk_f"][0]), 16)
                wgk_loads.on(act.dma_start(wgk[16:32, 1, :], A["w_gk_b"][0]), 16)
                j_vec[0].emptied_for(act)
                scol_ready.on(nc.scalar.activation(scol[:, :, 0], vcol("c", 0, KD), ACT.Silu))
                scol_ready.on(nc.scalar.activation(scol[:, :, 1], vcol("c_ctx", 0, KD), ACT.Silu))
                act.wait_ge(rows_loads.sem, 32)
                for t in range(NT + NTC):
                    if t:
                        rms_sum.wait(act)
                    rms_sum.on(nc.scalar.activation(junk[:], xtile(t), ACT.Square,
                                                    accum_out=stat[:, t:t + 1]))
                act.wait_ge(rms_mean.sem, 1)
                rms_root.on(nc.scalar.activation(stat[:, 16:22], stat[:, 8:14], ACT.Sqrt))
                act.wait_ge(mod_ready.sem, 3)
                for k in range(KD):
                    j = j_tr[k][0]
                    j.filled(act)
                    j.empty(nc.scalar.activation(hT[:, k, 0:T], bank(j.bank), ACT.Identity,
                                                 bias=mod1[:, k, 0:1], scale=amix[:, k, 0:1]))
                for i, j in enumerate(j_qk):
                    j.filled(act)
                    dst = qT[:, i, :] if i < 2 else kT[:, i - 2, 0:T]
                    j.empty(nc.scalar.activation(dst, bank(j.bank), ACT.Copy, scale=DK ** -0.5 if i < 2 else 1.0))
                for i, j in enumerate(j_kc):
                    j.filled(act)
                    j.empty(nc.scalar.activation(kT[:, i, T:], bank(j.bank, TC), ACT.Copy))
                for i, j in enumerate(j_g):
                    j.filled(act)
                    j.empty(nc.scalar.activation(sgT[:, i, :], bank(j.bank), ACT.Silu))

            @block.vector
            def _(dve):
                j_vec[0].filled(dve)
                j_vec[0].empty(nc.vector.tensor_copy(vec[:], bank(0, 3 * P)))
                dve.wait_ge(rms_sum.sem, NT + NTC)
                rms_mean.on(nc.vector.tensor_scalar(stat[:, 8:14], stat[:, 0:6], 1.0 / D, EPS, ALU.mult, ALU.add))
                dve.wait_ge(rms_root.sem, 1)
                dve_step.on(nc.vector.reciprocal(stat[:, 24:30], stat[:, 16:22]))
                dve_step.wait(dve)
                for t in range(NT + NTC):
                    xn_ready.on(nc.vector.tensor_scalar(xtile(t), xtile(t), stat[:, 24 + t:25 + t], None,
                                                        ALU.mult))
                for i, j in enumerate(j_rows):
                    j.filled(dve)
                    j.empty(nc.vector.tensor_copy(mod_rows[:, i * BANK:(i + 1) * BANK], bank(j.bank, BANK, 2)))
                j = j_mod[0]
                j.filled(dve)
                j.empty(nc.vector.tensor_tensor(
                    mod1[:], bank(1, 4 * KD).rearrange("p (f v) -> p f v", v=2),
                    vcol("b_ada", 0, 2 * KD).unsqueeze(2).to_broadcast([P, 2 * KD, 2]), ALU.add))
                j.emptied_for(dve)
                for v in range(2):
                    mod_ready.on(nc.vector.scalar_tensor_tensor(
                        out=amix[:, :, v], in0=mod1[:, KD:, v], scalar=1.0, in1=vcol("norm_mix_w", 0, KD),
                        op0=ALU.add, op1=ALU.mult))
                mod_ready.wait(dve)
                mod_ready.on(nc.vector.memset(stat[:, 60:61], 0.0))
                for k in range(KD):
                    j = j_tr[k][1]
                    j.filled(dve)
                    j.empty(nc.vector.tensor_scalar(hT[:, k, T:], bank(j.bank, TC), amix[:, k, 1:2],
                                                    mod1[:, k, 1:2], ALU.mult, ALU.add))
                for t, j in enumerate(j_v + j_vc):
                    j.filled(dve)
                    j.empty(nc.vector.tensor_copy(vtok[:, t, :], bank(j.bank)))
                j_r.filled(dve)
                j_r.empty(nc.vector.tensor_copy(rT[:, 0:T], bank(j_r.bank, T, 32)))
                j_rc.filled(dve)
                j_rc.empty(nc.vector.tensor_copy(rT[:, T:], bank(j_rc.bank, TC, 32)))
                for t, j in enumerate(j_pool):
                    j.filled(dve)
                    j.empty(nc.vector.tensor_copy(ptok[:, t, :], bank(j.bank)))

            @block.tensor
            def _(pe):
                vec_loads.wait(pe)
                for i in range(3):
                    mm = nc.tensor.transpose(ps[:, 0, i * P:(i + 1) * P], vrow[:, i, :], ident)
                j_vec[0].done(mm)
                pe.wait_ge(scol_ready.sem, 2)
                vector_rows(pe, j_rows)
                turn_vector_rows(pe, j_rows, j_mod[0], mod_rows)
                pe.wait_ge(xn_ready.sem, NT + NTC)
                for k in range(KD):
                    jx, jc = j_tr[k]
                    jx.open(pe)
                    for t in range(NT):
                        mm = nc.tensor.transpose(ps[:, jx.bank, t * P:(t + 1) * P], xtile(t)[:, k * P:(k + 1) * P], ident)
                    jx.done(mm)
                    jc.open(pe)
                    for t in range(NTC):
                        mm = nc.tensor.transpose(ps[:, jc.bank, t * P:(t + 1) * P],
                                                 xtile(NT + t)[:, k * P:(k + 1) * P], ident)
                    jc.done(mm)
                j_tr[-1][0].emptied_for(pe)
                j_tr[-1][1].emptied_for(pe)

                def tokens(t):
                    return slice(t * P, (t + 1) * P)

                tiles = [take(pe) for _ in range(4)]
                for k in range(KD):
                    w = tiles[k // 2][:, k % 2]
                    for i, j in enumerate(j_qk):
                        if k == 0:
                            j.open(pe)
                        mm = nc.tensor.matmul(bank(j.bank), w[:, i * P:(i + 1) * P], hT[:, k, 0:T],
                                              start=k == 0, stop=k == KD - 1)
                        if k == KD - 1:
                            j.done(mm)
                    for t, j in enumerate(j_v):
                        if k == 0:
                            j.open(pe)
                        mm = nc.tensor.matmul(bank(j.bank), hT[:, k, tokens(t)], w[:, 512:1024],
                                              start=k == 0, stop=k == KD - 1)
                        if k == KD - 1:
                            j.done(mm)
                for k in range(KD):
                    w = tiles[k // 2][:, k % 2]
                    for i, j in enumerate(j_kc):
                        if k == 0:
                            j.open(pe)
                        mm = nc.tensor.matmul(bank(j.bank, TC), w[:, (2 + i) * P:(3 + i) * P], hT[:, k, T:],
                                              start=k == 0, stop=k == KD - 1)
                        if k == KD - 1:
                            j.done(mm)
                    for t, j in enumerate(j_vc):
                        if k == 0:
                            j.open(pe)
                        mm = nc.tensor.matmul(bank(j.bank), hT[:, k, T + t * P:T + (t + 1) * P], w[:, 512:1024],
                                              start=k == 0, stop=k == KD - 1)
                        if k == KD - 1:
                            j.done(mm)
                    if k % 2 and k < KD - 1:
                        stream.release(mm)
                stream.owe()
                jobs = [(j, bank(j.bank), lambda k, w, kk, i=i: w[:, kk, i * P:(i + 1) * P],
                         lambda k, w, kk: hT[:, k, 0:T]) for i, j in enumerate(j_g)]
                jobs += [(j_r, bank(j_r.bank, T, 32), lambda k, w, kk: w[:, kk, 512:544],
                          lambda k, w, kk: hT[:, k, 0:T]),
                         (j_rc, bank(j_rc.bank, TC, 32), lambda k, w, kk: w[:, kk, 512:544],
                          lambda k, w, kk: hT[:, k, T:])]
                project(pe, 3, jobs)
                project(pe, 2, [(j, bank(j.bank), lambda k, w, kk, t=t: hT[:, k, tokens(t)],
                                 lambda k, w, kk: w[:, kk, :]) for t, j in enumerate(j_pool)])
        in_scope.close()
        g1b = sbuf("g1b", [P, D], scope=mix_scope)
        mixT = sbuf("mixT", [P, KD, T], scope=mix_scope)
        bc = sbuf("bc", [P, 4, T + TC], scope=mix_scope)
        scratch = ring[:, MIX_SLOTS:, :].rearrange("p s n -> p (s n)")
        W3 = T + TC
        zb = scratch[:, 0:4 * W3].rearrange("p (i n) -> p i n", i=4)
        scb = scratch[:, 3072:3072 + D].rearrange("p (k n) -> p k n", k=KD)
        pooled = scratch[:, 4096:4096 + 4 * T].rearrange("p (g n) -> p g n", g=4)
        DM = [(d, m) for d in range(2) for m in range(2)]

        j_z = [(psum.job(2 * i, "dve"), psum.job(2 * i + 1, "dve")) for i in range(4)]
        j_g1 = [psum.job(0, "dve"), psum.job(1, "dve")]
        j_rows2 = [psum.job(2 + i, "dve") for i in range(4)]
        j_g2 = [psum.job(6, "dve"), psum.job(7, "dve")]
        j_m2 = psum.job(2, "dve")
        mod2_rows = res[0:2, 0:2, :].rearrange("p t n -> p (t n)")
        j_pm = [psum.job(5 + g % 2, "act") for g in range(4)]
        j_pw = [psum.job((7, 0, 1, 2)[g], "act") for g in range(4)]
        row_loads = signal("row_loads")
        scb_ready = signal("scb_ready")
        gk_step = signal("gk_step")
        z_half = signal("z_half")

        with nc.Block() as block:
            @block.sync
            def _(sp):
                row_loads.on(sp.dma_start(g1b[:], A["b_ada_row"][0:1, 2 * D:3 * D].to_broadcast([P, D])), 16)
                row_loads.on(sp.dma_start(g2b[:], A["b_ada_row"][0:1, 5 * D:6 * D].to_broadcast([P, D])), 16)
                stream.load(sp, end_gates, MIX_SLOTS)

            @block.vector
            def _(dve):
                scb_ready.on(nc.vector.tensor_copy(scb, scol[:, :, 0].unsqueeze(2).to_broadcast([P, KD, P])))
                for i, (d, m) in enumerate(DM):
                    bias = vcol(("b_gk_f", "b_gk_b")[d], m)
                    for j, cols in zip(j_z[i], (slice(0, T), slice(T, W3))):
                        j.filled(dve)
                        j.empty(nc.vector.tensor_scalar(zb[:, i, cols], bank(j.bank, cols.stop - cols.start), bias, None,
                                                        ALU.add))
                dve.wait_ge(gk_step.sem, 1)
                z_half.on(nc.vector.tensor_scalar(zb, zb, 0.0, 1.0 / 16, ALU.min, ALU.mult))
                z_half.wait(dve)
                dve.wait_ge(gk_step.sem, 3)
                z_half.on(nc.vector.scalar_tensor_tensor(out=zb, in0=bc[:], scalar=-1.0 / 16, in1=zb, op0=ALU.mult,
                                                         op1=ALU.add))
                z_half.wait(dve)
                reset = cst[:, C_RESET:C_RESET + W3]
                for i, (d, m) in enumerate(DM):
                    step = -1 if d else 1
                    nc.vector.tensor_tensor_scan(bc[:, i, ::step], reset, zb[:, i, ::step], 0.0, ALU.mult, ALU.add)
                dve.wait_ge(row_loads.sem, 32)
                for half, j in enumerate(j_g1):
                    j.filled(dve)
                    cols = slice(half * BANK, (half + 1) * BANK)
                    j.empty(nc.vector.tensor_tensor(g1b[:, cols], bank(j.bank), g1b[:, cols], ALU.add))
                for i, j in enumerate(j_rows2):
                    j.filled(dve)
                    j.empty(nc.vector.tensor_copy(mod2_rows[:, i * BANK:(i + 1) * BANK], bank(j.bank, BANK, 2)))
                for half, j in enumerate(j_g2):
                    j.filled(dve)
                    cols = slice(half * BANK, (half + 1) * BANK)
                    j.empty(nc.vector.tensor_tensor(g2b[:, cols], bank(j.bank), g2b[:, cols], ALU.add))
                j_m2.filled(dve)
                j_m2.empty(nc.vector.tensor_tensor(
                    mod2[:], bank(j_m2.bank, 4 * KD).rearrange("p (f v) -> p f v", v=2),
                    vcol("b_ada", 3 * KD, 2 * KD).unsqueeze(2).to_broadcast([P, 2 * KD, 2]), ALU.add))
                j_m2.emptied_for(dve)
                dve_step.on(nc.vector.scalar_tensor_tensor(
                    out=mod2[:, KD:, 0], in0=mod2[:, KD:, 0], scalar=1.0, in1=vcol("norm_mlp_w", 0, KD),
                    op0=ALU.add, op1=ALU.mult))

            @block.scalar
            def _(act):
                j_z[-1][1].emptied_for(act)
                gk_step.on(nc.scalar.activation(bc[:], zb, ACT.Abs))
                gk_step.wait(act)
                gk_step.on(nc.scalar.activation(bc[:], bc[:], ACT.Exp, scale=-1.0))
                gk_step.wait(act)
                gk_step.on(nc.scalar.activation(bc[:], bc[:], ACT.Ln, bias=1.0))
                for g, j in enumerate(j_pm):
                    j.filled(act)
                    j.empty(nc.scalar.activation(pooled[:, g, :], bank(j.bank), ACT.Copy))
                for g, j in enumerate(j_pw):
                    j.filled(act)
                    j.empty(nc.scalar.activation(mixT[:, 4 + g, :], bank(j.bank), ACT.Copy, scale=vcol("pool_scale", g)))

            @block.tensor
            def _(pe):
                wgk_loads.wait(pe)
                for i, (d, m) in enumerate(DM):
                    for j, cols in zip(j_z[i], (slice(0, T), slice(T, W3))):
                        j.open(pe)
                        j.done(nc.tensor.matmul(bank(j.bank, cols.stop - cols.start), wgk[:, d, m * P:(m + 1) * P],
                                                rT[:, cols], start=True, stop=True))
                pe.wait_ge(scb_ready.sem, 1)

                def gate_row(jobs):
                    project(pe, 4, [(j, bank(j.bank), lambda k, w, kk: scb[:, k, :],
                                     lambda k, w, kk, i=i: w[:, kk, i * BANK:(i + 1) * BANK])
                                    for i, j in enumerate(jobs)])

                gate_row(j_g1)
                vector_rows(pe, j_rows2)
                gate_row(j_g2)
                turn_vector_rows(pe, j_rows2, j_m2, mod2_rows)
                for g, j in enumerate(j_pm):
                    w = take(pe)
                    j.open(pe)
                    for t in range(NT):
                        mm = nc.tensor.matmul(bank(j.bank), ptok[:, t, g * P:(g + 1) * P], w[:, t, :],
                                              start=t == 0, stop=t == NT - 1)
                        if t == 0:
                            stream.settle(mm)
                    j.done(mm)
                    stream.owe()
                w = take(pe)
                for g, j in enumerate(j_pw):
                    j_pm[g].emptied_for(pe)
                    j.open(pe)
                    j.done(nc.tensor.matmul(bank(j.bank), w[:, g, :], pooled[:, g, :], start=True, stop=True))
                stream.owe()
        def gset(i):
            at = i * 3072
            v = lambda a, n: scratch[:, at + a:at + a + n]
            return v(0, W3), v(W3, T), v(W3 + T, T), v(W3 + 2 * T, T), v(W3 + 3 * T, W3)

        sets = [gset(0), gset(1)]
        amat = [scratch[:, 6144 + i * D:6144 + (i + 1) * D].rearrange("p (h t n) -> p h t n", h=2, t=NT)
                for i in range(2)]
        states = [ptok[:].rearrange("p t n -> p (t n)")[:, 0:11 * DV].rearrange("p (s n) -> p s n", s=11),
                  res[:, 0:2, :].rearrange("p t n -> p (t n)")[:, 0:11 * DV].rearrange("p (s n) -> p s n", s=11)]
        onorm = res[:, 2:4, :].rearrange("p t n -> p (t n)").rearrange("p (t n) -> p t n", t=NT)
        decay = stat[:, 32:56].rearrange("p (b c) -> p b c", b=2)
        ohead = stat[:, 0:16]

        def order(d):
            xs, cs = list(range(NCH)), list(range(NCH, NCH + NCHC))
            return (cs + xs) if d == 0 else (cs[::-1] + xs[::-1])

        def u_place(c):
            return (c % 2, c // 2) if c < NCH else (2 + c % 2, (c - NCH) // 2)

        U_ORDER = [[2, 3, 1, 0], [3, 2, 0, 1]]
        jobs_gla = []
        for i in range(4):
            jt = [psum.job(4, "act"), psum.job(5, "act")]
            ja = [psum.job(6, "dve"), psum.job(7, "dve")]
            ju = {g: psum.job(4 + g, "dve") for g in U_ORDER[DM[i][0]]}
            jobs_gla.append((jt, ja, ju))
        j_o = [psum.job(t, "dve") for t in range(NT)]
        j_mix = [psum.job(4 + h, "dve") for h in range(H)]
        amat_zero = signal("amat_zero")
        shifted = signal("shifted")
        powers = signal("powers")
        scaled = signal("scaled")
        state_step = signal("state_step")
        o_done = signal("o_done")
        o_sq = signal("o_sq")
        o_sum = signal("o_sum")
        o_root = signal("o_root")
        o_inv = signal("o_inv")

        def kU_sq(t):
            return scratch[:, t * BANK:(t + 1) * BANK]

        zeros = sbuf("zeros", [P, BANK], scope=mix_scope)
        zero_ready = signal("zero_ready")
        rows_zeroed = signal("rows_zeroed")

        def chunk_view(ap, n):
            return ap.rearrange("p (c n) -> p c n", n=CHUNK)

        with nc.Block() as block:
            @block.sync
            def _(sp):
                stream.load(sp, end_gates, MIX_SLOTS)

            @block.gpsimd
            def _(pool):
                for a in amat:
                    amat_zero.on(nc.gpsimd.memset(a, 0.0))
                zero_ready.on(nc.gpsimd.memset(zeros[:], 0.0))
                zero_ready.wait(pool)
                rows_zeroed.on(pool.dma_start(
                    y_dram[E * CAP:, :].rearrange("r (h n) -> (r h) n", n=BANK).rearrange("(p a) n -> p a n", p=P),
                    zeros[:].unsqueeze(1).to_broadcast([P, XB * D // BANK, BANK])), 16)
                rows_zeroed.wait(pool)

            @block.vector
            def _(dve):
                def shift(i):
                    kU, qE, kE, qD, kUT = sets[i % 2]
                    d, m = DM[i]
                    b = bc[:, i, :].rearrange("p (c n) -> p c n", n=CHUNK)
                    last, mid = (CHUNK - 1, CHUNK // 2 - 1) if d == 0 else (0, CHUNK // 2)
                    if i >= 2:
                        dve.wait_ge(o_done.sem, 2 * (i - 1))
                    shifted.on(nc.vector.tensor_tensor(chunk_view(kU, W3), b,
                                                       b[:, :, last:last + 1].to_broadcast([P, 12, CHUNK]),
                                                       ALU.subtract))
                    shifted.on(nc.vector.tensor_tensor(chunk_view(qE, T), b[:, 0:NCH, :],
                                                       b[:, 0:NCH, mid:mid + 1].to_broadcast([P, NCH, CHUNK]),
                                                       ALU.subtract))

                def scale(i):
                    kU, qE, kE, qD, kUT = sets[i % 2]
                    d, m = DM[i]
                    dve.wait_ge(powers.sem, 5 * i + 5)
                    scaled.on(nc.vector.tensor_tensor(kU, kU, kT[:, m, :], ALU.mult))
                    scaled.on(nc.vector.tensor_tensor(kE, kE, kT[:, m, 0:T], ALU.mult))
                    scaled.on(nc.vector.tensor_tensor(qE, qE, qT[:, m, :], ALU.mult))
                    scaled.on(nc.vector.tensor_tensor(qD, qD, qT[:, m, :], ALU.mult))

                def recur(i):
                    d, m = DM[i]
                    jt, ja, ju = jobs_gla[i]
                    mask = cst[:, (C_MF, C_MB)[d]:(C_MF, C_MB)[d] + P].bitcast(U32)
                    for hh in range(2):
                        if i == 0:
                            dve.wait_ge(amat_zero.sem, 2)
                        if i % 2:
                            dve.wait_ge(o_done.sem, 2 * i)
                        ja[hh].filled(dve)
                        ja[hh].empty(nc.vector.copy_predicated(
                            amat[d][:, hh], mask.unsqueeze(1).to_broadcast([P, NT, P]),
                            bank(ja[hh].bank).rearrange("p (t n) -> p t n", t=NT)))
                    S = states[i % 2]
                    chunks = order(d)[:11]
                    for s, c in enumerate(chunks):
                        g, cc = u_place(c)
                        j = ju[g]
                        u = ps[:, j.bank, cc * DV:(cc + 1) * DV]
                        j.filled(dve)
                        if s == 0:
                            if i >= 2:
                                dve.wait_ge(o_done.sem, 2 * (i - 1))
                            ins = nc.vector.tensor_copy(S[:, 0, :], u)
                        else:
                            ins = nc.vector.scalar_tensor_tensor(
                                out=S[:, s, :], in0=S[:, s - 1, :], scalar=decay[:, i % 2, c:c + 1], in1=u,
                                op0=ALU.mult, op1=ALU.add)
                        later = [x for x in chunks[s + 1:] if u_place(x)[0] == g]
                        if later:
                            state_step.on(ins)
                            state_step.wait(dve)
                        else:
                            j.empty(ins)
                            j.emptied_for(dve)

                shift(0)
                shift(1)
                scale(0)
                for i in range(4):
                    if i + 1 < 4:
                        scale(i + 1)
                    recur(i)
                    if i + 2 < 4:
                        shift(i + 2)
                dve.wait_ge(o_sq.sem, 1)
                for t in range(NT):
                    dve.wait_ge(o_sq.sem, t + 1)
                    o_sum.on(nc.vector.tensor_reduce(ohead[:, 4 * t:4 * t + 4],
                                                     kU_sq(t).rearrange("p (h n) -> p h n", h=H), AX.X, ALU.add))
                o_sum.wait(dve)
                o_inv.on(nc.vector.tensor_scalar(ohead, ohead, 1.0 / DV, EPS, ALU.mult, ALU.add))
                dve.wait_ge(o_root.sem, 1)
                o_inv.on(nc.vector.reciprocal(ohead, ohead))
                o_inv.wait(dve)
                for t in range(NT):
                    j_o[t].empty(nc.vector.tensor_tensor(
                        onorm[:, t, :].rearrange("p (h n) -> p h n", h=H), bank(t).rearrange("p (h n) -> p h n", h=H),
                        ohead[:, 4 * t:4 * t + 4].unsqueeze(2).to_broadcast([P, H, DV]), ALU.mult))
                for h, j in enumerate(j_mix):
                    j.filled(dve)
                    j.empty(nc.vector.scalar_tensor_tensor(out=mixT[:, h, :], in0=bank(j.bank),
                                                           scalar=vcol("gla_norm_w"), in1=sgT[:, h, :],
                                                           op0=ALU.mult, op1=ALU.mult))

            @block.scalar
            def _(act):
                def power(i):
                    kU, qE, kE, qD, kUT = sets[i % 2]
                    d, m = DM[i]
                    last = CHUNK - 1 if d == 0 else 0
                    act.wait_ge(shifted.sem, 2 * i + 2)
                    if i >= 2:
                        jobs_gla[i - 2][2][U_ORDER[DM[i - 2][0]][-1]].emptied_for(act)
                    powers.on(nc.scalar.activation(decay[:, i % 2, :],
                                                   bc[:, i, :].rearrange("p (c n) -> p c n", n=CHUNK)[:, :, last],
                                                   ACT.Exp))
                    powers.on(nc.scalar.activation(kU, kU, ACT.Exp, scale=-1.0))
                    powers.on(nc.scalar.activation(kE, qE, ACT.Exp, scale=-1.0))
                    powers.wait(act)
                    powers.on(nc.scalar.activation(qE, qE, ACT.Exp))
                    powers.on(nc.scalar.activation(qD, bc[:, i, 0:T], ACT.Exp))

                def turned(i):
                    kU, qE, kE, qD, kUT = sets[i % 2]
                    for g, j in enumerate(jobs_gla[i][0]):
                        j.filled(act)
                        n = (NT, NTC)[g] * P
                        j.empty(nc.scalar.activation(kUT[:, g * T:g * T + n], bank(j.bank, n), ACT.Copy))

                power(0)
                power(1)
                for i in range(4):
                    turned(i)
                    if i + 2 < 4:
                        power(i + 2)
                act.wait_ge(o_done.sem, 6)
                for t in range(NT):
                    j_o[t].filled(act)
                    o_sq.on(nc.scalar.activation(kU_sq(t), bank(t), ACT.Square))
                act.wait_ge(o_inv.sem, 1)
                o_root.on(nc.scalar.activation(ohead, ohead, ACT.Sqrt))

            @block.tensor
            def _(pe):
                for i in range(4):
                    kU, qE, kE, qD, kUT = sets[i % 2]
                    d, m = DM[i]
                    jt, ja, ju = jobs_gla[i]
                    pe.wait_ge(scaled.sem, 4 * i + 4)
                    for g, j in enumerate(jt):
                        j.open(pe)
                        for t in range((NT, NTC)[g]):
                            mm = nc.tensor.transpose(ps[:, j.bank, t * P:(t + 1) * P],
                                                     kU[:, g * T + t * P:g * T + (t + 1) * P], ident)
                        j.done(mm)
                    for hh, j in enumerate(ja):
                        j.open(pe)
                        rows_h = slice(64 * hh, 64 * hh + 64)
                        for t in range(NT):
                            mm = nc.tensor.matmul(ps[:, j.bank, t * P:(t + 1) * P], kE[rows_h, t * P:(t + 1) * P],
                                                  qE[rows_h, t * P:(t + 1) * P], start=True, stop=True)
                        j.done(mm)
                    jt[0].emptied_for(pe)
                    jt[1].emptied_for(pe)
                    for g in U_ORDER[d]:
                        j = ju[g]
                        j.open(pe)
                        for c in [c for c in range(NCH + NCHC) if u_place(c)[0] == g]:
                            t, cc = c // 2, u_place(c)[1]
                            rows_c = slice(64 * (c % 2), 64 * (c % 2) + 64)
                            for hh in range(2):
                                head = 2 * m + hh
                                mm = nc.tensor.matmul(ps[64 * hh:64 * hh + 64, j.bank, cc * DV:(cc + 1) * DV],
                                                      kUT[rows_c, t * P + 64 * hh:t * P + 64 * hh + 64],
                                                      vtok[rows_c, t, head * DV:(head + 1) * DV], start=True, stop=True)
                        j.done(mm)
                    ja[0].emptied_for(pe)
                    ja[1].emptied_for(pe)
                    for j in ju.values():
                        j.emptied_for(pe)
                    pos = {c: s for s, c in enumerate(order(d))}
                    for hh in range(2):
                        head = 2 * m + hh
                        rows_h = slice(64 * hh, 64 * hh + 64)
                        cols = slice(head * DV, (head + 1) * DV)
                        if i or hh:
                            pe.wait_ge(o_done.sem, 2 * i + hh)
                        for t in range(NT):
                            if i == 0 and hh == 0:
                                j_o[t].open(pe)
                            nc.tensor.matmul(ps[:, t, cols], amat[d][:, hh, t, :], vtok[:, t, cols],
                                             start=i == 0 and hh == 0, stop=False, skip_group_check=True)
                            for half in range(2):
                                c = 2 * t + half
                                mm = nc.tensor.matmul(ps[64 * half:64 * half + 64, t, cols],
                                                      qD[rows_h, c * CHUNK:(c + 1) * CHUNK],
                                                      states[i % 2][rows_h, pos[c] - 1, :],
                                                      start=False, stop=i == 3, skip_group_check=True)
                            if i == 3 and hh:
                                j_o[t].done(mm)
                        if i < 3 or hh == 0:
                            o_done.on(mm)
                for t in range(NT):
                    j_o[t].emptied_for(pe)
                for h, j in enumerate(j_mix):
                    j.open(pe)
                    for t in range(NT):
                        mm = nc.tensor.transpose(ps[:, j.bank, t * P:(t + 1) * P], onorm[:, t, h * P:(h + 1) * P], ident)
                    j.done(mm)
        hT2 = scratch[:, 0:KD * T].rearrange("p (k n) -> p k n", k=KD)
        xnt = scratch[:, KD * T:2 * KD * T].rearrange("p (t n) -> p t n", t=NT)
        prod = qT[:]
        sq2 = kT[:].rearrange("p a n -> p (a n)")[:, 0:D]
        rt = sgT[:].rearrange("p h n -> p (h n)")
        oh = rt[:, 0:512].rearrange("p (t k e) -> p t k e", t=NT, k=TOPK)
        ohw = rt[:, 512:1024].rearrange("p (t k e) -> p t k e", t=NT, k=TOPK)
        logit = rt[:, 1024:1152].rearrange("p (t e) -> p t e", t=NT)
        member = rt[:, 1152:1280].rearrange("p (t e) -> p t e", t=NT)
        rowof = rt[:, 1280:1408].rearrange("p (t e) -> p t e", t=NT)
        top8 = rt[:, 1408:1440].rearrange("p (t k) -> p t k", t=NT)
        idx8 = rt[:, 1440:1472].bitcast(U32).rearrange("p (t k) -> p t k", t=NT)
        idxf = rt[:, 1472:1488].rearrange("p (t k) -> p t k", t=NT)
        ex = rt[:, 1488:1504].rearrange("p (t k) -> p t k", t=NT)
        destf = rt[:, 1504:1520].rearrange("p (t k) -> p t k", t=NT)
        esum = rt[:, 1520:1524]
        brb = rt[:, 1536:1568]
        count = rt[:, 1568:1600]
        extra, tmp32 = rt[:, 1600:1632], rt[:, 1632:1664]
        xend, xstart = xends[:, 0, :], xends[:, 1, :]

        j_out = {(t, h): psum.job(4 * h + t, "dve") for h in range(2) for t in range(NT)}
        j_h2 = [psum.job(k, "act") for k in range(KD)]
        j_log = psum.job(0, "dve")
        j_rank = psum.job(1, "dve")
        x_back = signal("x_back")
        res_ready = signal("res_ready")
        n2_sum = signal("n2_sum")
        n2_mean = signal("n2_mean")
        n2_root = signal("n2_root")
        xn2_ready = signal("xn2_ready")
        xn2_stored = signal("xn2_stored")
        route = signal("route")
        expd = signal("expd")
        expd_done = signal("expd_done")
        member_ready = signal("member_ready")
        posm_zero = signal("posm_zero")

        with nc.Block() as block:
            @block.sync
            def _(sp):
                x_back.on(sp.dma_start(res[:], A["x"][0].rearrange("(t p) n -> p t n", p=P)), 16)
                x_back.on(sp.dma_start(brb, A["b_router"][0:1, :].to_broadcast([P, E])), 16)
                stream.load(sp, end_mix, MIX_SLOTS)
                sp.wait_ge(xn2_ready.sem, NT)
                xn2_stored.on(sp.dma_start(xn_dram.rearrange("(t p) n -> p t n", p=P), xnt), 16)
                xn2_stored.wait(sp)

            @block.gpsimd
            def _(pool):
                posm_zero.on(nc.gpsimd.memset(posm[:], 0.0))

            @block.scalar
            def _(act):
                for t in range(NT):
                    act.wait_ge(res_ready.sem, 4 + t + 1)
                    if t:
                        n2_sum.wait(act)
                    n2_sum.on(nc.scalar.activation(sq2, res[:, t, :], ACT.Square, accum_out=stat[:, t:t + 1]))
                act.wait_ge(n2_mean.sem, 1)
                n2_root.on(nc.scalar.activation(stat[:, 4:8], stat[:, 4:8], ACT.Sqrt))
                for k, j in enumerate(j_h2):
                    j.filled(act)
                    j.empty(nc.scalar.activation(hT2[:, k, :], bank(j.bank), ACT.Identity, bias=mod2[:, k, 0:1],
                                                 scale=mod2[:, KD + k, 0:1]))
                act.wait_ge(expd.sem, 1)
                expd_done.on(nc.scalar.activation(ex, ex, ACT.Exp))

            @block.vector
            def _(dve):
                dve.wait_ge(x_back.sem, 32)
                for n, ((t, h), j) in enumerate(j_out.items()):
                    cols = slice(h * BANK, (h + 1) * BANK)
                    j.filled(dve)
                    if n >= 2:
                        dve.wait_ge(res_ready.sem, n - 1)
                    j.empty(nc.vector.tensor_tensor(prod[:, n % 2, :], bank(j.bank), g1b[:, cols], ALU.mult))
                    j.emptied_for(dve)
                    res_ready.on(nc.vector.tensor_tensor(res[:, t, cols], res[:, t, cols], prod[:, n % 2, :], ALU.add))
                dve.wait_ge(n2_sum.sem, NT)
                n2_mean.on(nc.vector.tensor_scalar(stat[:, 4:8], stat[:, 0:4], 1.0 / D, EPS, ALU.mult, ALU.add))
                dve.wait_ge(n2_root.sem, 1)
                n2_mean.on(nc.vector.reciprocal(stat[:, 4:8], stat[:, 4:8]))
                n2_mean.wait(dve)
                for t in range(NT):
                    xn2_ready.on(nc.vector.tensor_scalar(xnt[:, t, :], res[:, t, :], stat[:, 4 + t:5 + t], None, ALU.mult))

                def step(ins):
                    route.on(ins)
                    route.wait(dve)

                j_log.filled(dve)
                j_log.empty(nc.vector.tensor_tensor(
                    logit, bank(j_log.bank, NT * E).rearrange("p (t e) -> p t e", t=NT),
                    brb.unsqueeze(1).to_broadcast([P, NT, E]), ALU.add))
                j_log.emptied_for(dve)
                for t in range(NT):
                    step(nc.vector.max(top8[:, t, :], logit[:, t, :]))
                    step(nc.vector.max_index(idx8[:, t, :], top8[:, t, :], logit[:, t, :]))
                expd.on(nc.vector.tensor_tensor(ex, top8[:, :, 0:TOPK], top8[:, :, 0:1].to_broadcast([P, NT, TOPK]),
                                                ALU.subtract))
                step(nc.vector.tensor_copy(idxf, idx8[:, :, 0:TOPK]))
                step(nc.vector.tensor_tensor(
                    oh.rearrange("p t k e -> p (t k) e"),
                    cst[:, C_IOTA32:C_IOTA32 + E].unsqueeze(1).to_broadcast([P, NT * TOPK, E]),
                    idxf.rearrange("p t k -> p (t k)").unsqueeze(2).to_broadcast([P, NT * TOPK, E]), ALU.is_equal))
                member_ready.on(nc.vector.tensor_reduce(member, oh.rearrange("p t k e -> p t e k"), AX.X, ALU.add))
                dve.wait_ge(expd_done.sem, 1)
                step(nc.vector.tensor_reduce(esum, ex, AX.X, ALU.add))
                step(nc.vector.reciprocal(esum, esum))
                step(nc.vector.tensor_tensor(wk[:], ex, esum.unsqueeze(2).to_broadcast([P, NT, TOPK]), ALU.mult))
                step(nc.vector.tensor_tensor(
                    ohw.rearrange("p t k e -> p (t k) e"), oh.rearrange("p t k e -> p (t k) e"),
                    wk[:].rearrange("p t k -> p (t k)").unsqueeze(2).to_broadcast([P, NT * TOPK, E]), ALU.mult))
                step(nc.vector.tensor_reduce(wtok[:], ohw.rearrange("p t k e -> p t e k"), AX.X, ALU.add))
                rank = bank(j_rank.bank, NT * E).rearrange("p (t e) -> p t e", t=NT)
                j_rank.filled(dve)
                dve.wait_ge(posm_zero.sem, 1)
                step(nc.vector.scalar_tensor_tensor(out=posm[:, :, 0:E], in0=rank, scalar=1.0, in1=member, op0=ALU.add,
                                                    op1=ALU.mult))
                step(nc.vector.tensor_copy(count, ps[:, j_rank.bank, NT * E:(NT + 1) * E]))
                step(nc.vector.tensor_scalar(extra, count, float(CAP), None, ALU.is_gt))
                for b in (2, 3):
                    step(nc.vector.scalar_tensor_tensor(out=extra, in0=count, scalar=float(b * CAP), in1=extra,
                                                        op0=ALU.is_gt, op1=ALU.add))
                step(nc.vector.tensor_tensor_scan(xend, ones[:, 0:E], extra, 0.0, ALU.mult, ALU.add))
                step(nc.vector.tensor_tensor(xstart, xend, extra, ALU.subtract))
                iota = cst[:, C_IOTA32:C_IOTA32 + E]
                step(nc.vector.tensor_tensor(tmp32, xstart, iota, ALU.subtract))
                step(nc.vector.tensor_scalar(tmp32, tmp32, float(E - 1), float(CAP), ALU.add, ALU.mult))
                step(nc.vector.scalar_tensor_tensor(out=rowof, in0=rank, scalar=float(CAP),
                                                    in1=tmp32.unsqueeze(1).to_broadcast([P, NT, E]), op0=ALU.is_ge,
                                                    op1=ALU.mult))
                j_rank.empty(nc.vector.tensor_tensor(rowof, rowof, rank, ALU.add))
                j_rank.emptied_for(dve)
                step(nc.vector.scalar_tensor_tensor(
                    out=rowof, in0=iota.unsqueeze(1).to_broadcast([P, NT, E]), scalar=float(CAP), in1=rowof,
                    op0=ALU.mult, op1=ALU.add))
                for t in range(NT):
                    nc.vector.tensor_tensor(ohw[:, t], oh[:, t], rowof[:, t:t + 1, :].to_broadcast([P, TOPK, E]),
                                            ALU.mult).then_inc(route.sem, 1)
                route.n += NT
                route.wait(dve)
                step(nc.vector.tensor_reduce(destf, ohw, AX.X, ALU.add))
                step(nc.vector.tensor_copy(dest[:], destf.rearrange("p t k -> p (t k)")))

            @block.tensor
            def _(pe):
                project(pe, 4, [(j, bank(j.bank), lambda k, w, kk, t=t: mixT[:, k, t * P:(t + 1) * P],
                                 lambda k, w, kk, h=h: w[:, kk, h * BANK:(h + 1) * BANK])
                                for (t, h), j in j_out.items()])
                pe.wait_ge(xn2_ready.sem, NT)
                for k, j in enumerate(j_h2):
                    j.open(pe)
                    for t in range(NT):
                        mm = nc.tensor.transpose(ps[:, j.bank, t * P:(t + 1) * P], xnt[:, t, k * P:(k + 1) * P], ident)
                        if k == 0 and t == 0:
                            stream.settle(mm)
                    j.done(mm)
                j_h2[-1].emptied_for(pe)
                w = take(pe)
                j_log.open(pe)
                for t in range(NT):
                    for k in range(KD):
                        mm = nc.tensor.matmul(ps[:, j_log.bank, t * E:(t + 1) * E], hT2[:, k, t * P:(t + 1) * P],
                                              w[:, k, :], start=k == 0, stop=k == KD - 1)
                j_log.done(mm)
                stream.owe()
                pe.wait_ge(member_ready.sem, 1)
                j_rank.open(pe)
                for t in range(NT + 1):
                    for u in range(min(t, NT - 1) + 1):
                        left = cst[:, C_TRI:C_TRI + P] if u == t else ones
                        mm = nc.tensor.matmul(ps[:, j_rank.bank, t * E:(t + 1) * E], left, member[:, u, :],
                                              start=u == 0, stop=u == min(t, NT - 1))
                        if t == 0:
                            stream.settle(mm)
                j_rank.done(mm)
        mix_scope.close()

        moe_scope = ctx.enter_context(ExitStack())
        bgu = sbuf("bgu", [3 * E, 2 * FF], scope=moe_scope)
        bparts = sbuf("bparts", [3 * E, 2 * FF], BF16, scope=moe_scope)
        xe = sbuf("xe", [P, D], scope=moe_scope)
        xeT = sbuf("xeT", [P, KD, P], scope=moe_scope)
        gate = sbuf("gate", [P, FF], scope=moe_scope)
        up = sbuf("up", [P, FF], scope=moe_scope)
        sig = sbuf("sig", [P, FF], scope=moe_scope)
        aT = sbuf("aT", [P, KD, P], scope=moe_scope)
        ysb = sbuf("ysb", [P, D], scope=moe_scope)
        onehot = sbuf("onehot", [P, NT, P], scope=moe_scope)
        sel = sbuf("sel", [3 * E, P], BF16, scope=moe_scope)
        idx = sbuf("idx", [P, 1], U32, scope=moe_scope)
        mark = sbuf("mark", [P, 1], scope=moe_scope)
        xval = sbuf("xval", [P, 2, XB], scope=moe_scope)
        ind, ind2 = (sbuf(f"ind{i}", [P, XB, E], scope=moe_scope)[:] for i in range(2))
        indw = sbuf("indw", [P, NT, XB, E], scope=moe_scope)[:]
        listing = signal("listing")
        iota1 = cst[:, C_IOTA1:C_IOTA1 + P]
        ident3 = cst[0:3 * E, C_ID3:C_ID3 + E + 1]
        Y0 = 4

        def dve_onehot(dve, S, pos):
            for t in range(NT):
                ins = nc.vector.tensor_scalar(onehot[:, t, :], iota1, pos(t), None, ALU.is_equal)
            ins.then_inc(S.onehot_ready, 1)

        def dve_ids(dve, S):
            nc.vector.tensor_copy(idx[:], ps[:, Y0, 0:1]).then_inc(S.ids_read, 1)

        def dve_sel(dve, S, column):
            nc.vector.tensor_scalar(sel[:], ones[0:3 * E, :], column, None, ALU.mult).then_inc(S.sel_ready, 1)

        def pe_ids(pe, S, settle=False):
            for t in range(NT):
                mm = nc.tensor.matmul(ps[:, Y0, 0:1], onehot[:, t, :], cst[:, C_TOK + t:C_TOK + t + 1],
                                      start=t == 0, stop=t == NT - 1)
            mm.then_inc(S.ids_done, 1)

        def pe_turn(pe, signal_, src, first=None):
            for k in range(KD):
                mm = nc.tensor.transpose(ps[:, 6 + k // 4, (k % 4) * P:(k % 4 + 1) * P], src[:, k * P:(k + 1) * P], ident)
                if k == 0 and first:
                    mm.then_inc(first, 1)
                if k % 4 == 3:
                    mm.then_inc(signal_, 1)

        def pool_gather(pool, S):
            nc.gpsimd.indirect_dma_start(xe[:], None, xn_dram, bass.IndirectOffsetOnAxis(ap=idx[:], axis=0)) \
                .then_inc(S.gathered, 16)

        def act_modulate(act, S):
            for k in range(KD):
                nc.scalar.activation(xeT[:, k, :], ps[:, 6 + k // 4, (k % 4) * P:(k % 4 + 1) * P], ACT.Identity,
                                     bias=mod2[:, k, 0:1], scale=mod2[:, KD + k, 0:1]).then_inc(S.xeT_read, 1)

        def pass_on(pool, S, n):
            pool.wait_ge(S.marked, n)
            nc.gpsimd.tensor_tensor(mark[:], ident[:, 0:1], ident[:, 0:1], ALU.mult).then_inc(S.marked, 1)

        M = Expert(*[sem(f"moe_{name}") for name in EXPERT_SIGNALS])
        consts = {"w_ready": [0] * SLOTS}
        for m in range(SLOTS):
            slot, _, _, landed, _, _ = stream.tiles[moe0 + m]
            consts["w_ready"][slot] = landed - 16
        bgu_loaded = signal("bgu_loaded")
        parted = signal("parted")
        rest = signal("rest")
        second, third = slice(E, 2 * E), slice(2 * E, 3 * E)

        with nc.Block() as block:
            @block.sync
            def _(sp):
                for part in range(3):
                    bgu_loaded.on(sp.dma_start(bgu[part * E:(part + 1) * E, :], A["b_gu"][0]), 16)
                while stream.loaded < moe0 + SLOTS:
                    slot, _, dmas, _, before, _ = stream.tiles[stream.loaded]
                    if before >= 0 and before >= end_mix - SLOTS:
                        sp.wait_ge(stream.used, before + 1)
                    for dst, src in dmas:
                        sp.dma_start(dst, src).then_inc(stream.ready[slot], 16)
                    stream.loaded += 1
                with sp.Fori(0, E - 2) as i:
                    for jj in range(SLOTS):
                        ahead, j = divmod(4 + jj, 12)
                        slot, view = stream.tiles[moe0 + SLOTS + jj][0:2]
                        sp.wait_ge(stream.used, 12 * i + (moe0 + 1 + jj))
                        if j < 8:
                            src = w_gu[i + (1 + ahead), j * P:(j + 1) * P, :]
                        else:
                            src = w_down[i + ahead, (j - 8) * 2 * P:(j - 7) * 2 * P, :].rearrange("(k p) n -> p k n", p=P)
                        sp.dma_start(view, src).then_inc(stream.ready[slot], 16)
                stream.loaded = moe0 + SLOTS + 12 * (E - 2)
                stream.load(sp, end_moe)

            @block.gpsimd
            def _(pool):
                nc.gpsimd.memset(mark[:], 0.0).then_inc(M.marked, 1)
                for e in range(2):
                    pool.wait_ge(M.ids_read, e + 1)
                    if e:
                        pool.wait_ge(M.xT_done, 2)
                    pool_gather(pool, M)

                def block_step(e):
                    pool.wait_ge(M.ids_read, e + 3)
                    pool.wait_ge(M.xT_done, e * 2 + 4)
                    pass_on(pool, M, e + 1)
                    pool_gather(pool, M)

                block_step(0)
                with pool.Fori(0, E - 1) as i:
                    block_step(i + 1)

            @block.scalar
            def _(act):
                nc.scalar.copy(ysb[:, 0:1], ident[:, 0:1]).then_inc(M.y_read, 2)
                nc.scalar.copy(ysb[:, 1:2], ident[:, 0:1]).then_inc(M.y_stored, 16)
                act.wait_ge(M.y_read, 2)
                act.wait_ge(M.y_stored, 16)
                act.wait_ge(bgu_loaded.sem, 48)
                parted.on(nc.scalar.copy(bparts[:], bgu[:]))
                act.wait_ge(M.xT_done, 2)
                act_modulate(act, M)
                act.wait_ge(rest.sem, 2)
                parted.on(nc.scalar.copy(bparts[third], bgu[third]))
                parted.on(nc.scalar.copy(bparts[second], bgu[second]))
                act.wait_ge(rest.sem, 3)
                parted.on(nc.scalar.copy(bparts[third], bgu[third]))

                def block_step(e, first):
                    act.wait_ge(M.gu_read, e * 2 + 1)
                    if not first:
                        act.wait_ge(M.act_ready, e)
                    nc.scalar.activation(sig[:], gate[:], ACT.Sigmoid, scale=1.702).then_inc(M.sig_ready, 1)
                    act.wait_ge(M.xT_done, e * 2 + 4)
                    act_modulate(act, M)
                    if not first:
                        store(e)

                def store(e):
                    act.wait_ge(M.y_stored, e * 16)
                    for h in range(2):
                        act.wait_ge(M.y_done, e * 2 - 1 + h)
                        nc.scalar.activation(ysb[:, h * BANK:(h + 1) * BANK], bank(Y0 + h), ACT.Copy) \
                            .then_inc(M.y_read, 1)
                    act.wait_ge(M.y_read, e * 2 + 2)
                    act.dma_start(row_blocks[e - 1], ysb[:]).then_inc(M.y_stored, 16)

                block_step(0, True)
                with act.Fori(0, E - 1) as i:
                    block_step(i + 1, False)
                store(E)
                act.wait_ge(M.y_stored, 16 * (E + 1))

            @block.vector
            def _(dve):
                for e in range(3):
                    if e:
                        dve.wait_ge(M.ids_done, e)
                    dve_onehot(dve, M, lambda t: posm[:, t, e:e + 1])
                    if e < 2:
                        dve.wait_ge(M.ids_done, e + 1)
                        if e:
                            dve.wait_ge(M.gathered, 16 * e)
                        dve_ids(dve, M)
                dve_sel(dve, M, ident3[:, 0:1])
                dve.wait_ge(parted.sem, 1)
                for part in (second, third):
                    rest.on(nc.vector.tensor_tensor(bgu[part], bgu[part], bparts[part], ALU.subtract))
                dve.wait_ge(parted.sem, 2)
                rest.on(nc.vector.tensor_tensor(bgu[third], bgu[third], bparts[third], ALU.subtract))

                def block_step(e):
                    dve.wait_ge(M.ids_done, e + 3)
                    dve.wait_ge(M.gathered, e * 16 + 32)
                    dve_ids(dve, M)
                    dve_onehot(dve, M, lambda t: posm[:, t, bass.ds(e + 3, 1)])
                    dve.wait_ge(M.gate_done, e + 1)
                    nc.vector.tensor_scalar(gate[:].rearrange("p (b n) -> p b n", b=2), ps[:, 0:2, :], 7.0, None,
                                            ALU.min).then_inc(M.gu_read, 1)
                    dve.wait_ge(M.up_done, e + 1)
                    nc.vector.tensor_scalar(up[:].rearrange("p (b n) -> p b n", b=2), ps[:, 2:4, :], 7.0, -7.0, ALU.min,
                                            ALU.max).then_inc(M.gu_read, 1)
                    dve_sel(dve, M, ident3[:, e + 1:e + 2] if isinstance(e, int) else ident3[:, bass.ds(e + 1, 1)])
                    dve.wait_ge(M.gu_read, e * 2 + 2)
                    nc.vector.scalar_tensor_tensor(out=up[:], in0=up[:], scalar=1.0, in1=gate[:], op0=ALU.add,
                                                   op1=ALU.mult).then_inc(M.ug_ready, 1)
                    dve.wait_ge(M.ug_ready, e + 1)
                    dve.wait_ge(M.sig_ready, e + 1)
                    nc.vector.tensor_tensor(up[:], up[:], sig[:], ALU.mult).then_inc(M.act_ready, 1)
                    for h in range(2):
                        dve.wait_ge(M.aT_done, e * 2 + 1 + h)
                        nc.vector.tensor_copy(aT[:, 4 * h:4 * h + 4, :].rearrange("p k n -> p (k n)"), bank(6 + h)) \
                            .then_inc(M.aT_read, 1)

                def step(ins):
                    listing.on(ins)
                    listing.wait(dve)

                block_step(0)
                xi = cst[:, C_XI:C_XI + XB].unsqueeze(2).to_broadcast([P, XB, E])
                step(nc.vector.tensor_tensor(ind, xi, xstart.unsqueeze(1).to_broadcast([P, XB, E]), ALU.is_ge))
                step(nc.vector.tensor_tensor(ind2, xi, xend.unsqueeze(1).to_broadcast([P, XB, E]), ALU.is_lt))
                step(nc.vector.tensor_tensor(ind, ind, ind2, ALU.mult))
                step(nc.vector.tensor_tensor(ind2, ind, cst[:, C_IOTA32:C_IOTA32 + E].unsqueeze(1)
                                             .to_broadcast([P, XB, E]), ALU.mult))
                step(nc.vector.tensor_reduce(xval[:, 0, :], ind2, AX.X, ALU.add))
                step(nc.vector.tensor_tensor(ind2, xi, xstart.unsqueeze(1).to_broadcast([P, XB, E]), ALU.subtract))
                step(nc.vector.scalar_tensor_tensor(out=ind2, in0=ind2, scalar=1.0, in1=ind, op0=ALU.add, op1=ALU.mult))
                step(nc.vector.tensor_reduce(xval[:, 1, :], ind2, AX.X, ALU.add))
                for t in range(NT):
                    nc.vector.tensor_tensor(indw[:, t], ind, posm[:, t, 0:E].unsqueeze(1).to_broadcast([P, XB, E]),
                                            ALU.mult).then_inc(listing.sem, 1)
                listing.n += NT
                listing.wait(dve)
                step(nc.vector.tensor_reduce(posx[:], indw, AX.X, ALU.add))
                step(nc.vector.scalar_tensor_tensor(
                    out=posx[:], in0=xval[:, 1:2, :].to_broadcast([P, NT, XB]), scalar=-float(CAP), in1=posx[:],
                    op0=ALU.mult, op1=ALU.add))
                step(nc.vector.tensor_copy(xlist[:, 0:XB], xval[:, 0, :]))
                step(nc.vector.tensor_copy(xlist[:, XB:], xend[:, E - 1:E]))
                with dve.Fori(0, E - 1) as i:
                    block_step(i + 1)

            @block.tensor
            def _(pe):
                def tile(m, turn):
                    slot, view = stream.tiles[moe0 + m][0:2]
                    pe.wait_ge(stream.ready[slot], turn * 16 + (consts["w_ready"][slot] + 16 * (m // SLOTS + 1)))
                    return view

                for e in range(2):
                    pe.wait_ge(M.onehot_ready, e + 1)
                    if e:
                        pe.wait_ge(M.ids_read, e)
                    pe_ids(pe, M)
                    if e == 0:
                        pe.wait_ge(M.gathered, 16)
                        pe_turn(pe, M.xT_done, xe)

                def down(e, m0, turn):
                    pe.wait_ge(M.ids_read, e + 3 if not (isinstance(e, int) and e == E) else E + 2)
                    pe.wait_ge(M.y_read, e * 2)
                    pe.wait_ge(M.aT_read, e * 2)
                    for j in range(4):
                        w = tile(m0 + j, turn)
                        for kk in range(2):
                            k = 2 * j + kk
                            for h in range(2):
                                mm = nc.tensor.matmul(bank(Y0 + h), aT[:, k, :], w[:, kk, h * BANK:(h + 1) * BANK],
                                                      start=k == 0, stop=k == KD - 1)
                                if k == KD - 1:
                                    mm.then_inc(M.y_done, 1)
                        if j < 3:
                            mm.then_inc(stream.used, 1)

                def block_step(e, m0, turn, first):
                    pe.wait_ge(M.xeT_read, e * 8 + 8)
                    if not first:
                        pe.wait_ge(M.gu_read, e * 2)
                    for k in range(KD):
                        w = tile(m0 + k, turn)
                        for b in range(4):
                            mm = nc.tensor.matmul(bank(b), xeT[:, k, :], w[:, b * BANK:(b + 1) * BANK], start=k == 0,
                                                  stop=False)
                        if k < KD - 1:
                            mm.then_inc(stream.used, 1)
                        if k == 0:
                            pe.wait_ge(M.onehot_ready, e + 3)
                            if not first:
                                pe.wait_ge(M.y_read, e * 2)
                            pe_ids(pe, M)
                    if first:
                        parted.wait(pe)
                    pe.wait_ge(M.sel_ready, e + 1)
                    for b in range(4):
                        mm = nc.tensor.matmul(bank(b), sel[:], bparts[:, b * BANK:(b + 1) * BANK], start=False, stop=True)
                        if b % 2:
                            mm.then_inc((M.gate_done, M.up_done)[b // 2], 1)
                    pe.wait_ge(M.gathered, e * 16 + 32)
                    if not first:
                        pe.wait_ge(M.aT_read, e * 2)
                    pe_turn(pe, M.xT_done, xe, first=stream.used)
                    if not first:
                        down(e, m0 + 8, turn)
                    pe.wait_ge(M.act_ready, e + 1)
                    pe.wait_ge(M.xeT_read, e * 8 + 16)
                    pe_turn(pe, M.aT_done, up, first=None if first else stream.used)

                block_step(0, 0, 0, True)
                with pe.Fori(0, E - 1) as i:
                    block_step(i + 1, 8, i, False)
                down(E, 8 + 12 * (E - 1), 0)
                stream.taken = end_moe
                stream.owe()

        xw = sbuf("xw", [P, 2, SLOT], scope=moe_scope)
        X = Expert(*[sem(f"extra_{name}") for name in EXPERT_SIGNALS])
        x_ready = [sem("x_ready0"), sem("x_ready1")]
        x_used = sem("x_used")

        def extra_blocks(eng, body):
            n = eng.value_load(xlist[0:1, XB:XB + 1], min_val=0, max_val=XB)
            with eng.If(n > 0):
                with eng.Fori(0, XB) as i:
                    body(i)

        def listed(eng, i):
            return eng.value_load(xlist[0:1, bass.ds(i, 1)], min_val=0, max_val=E - 1)

        with nc.Block() as block:
            @block.sync
            def _(sp):
                def body(i):
                    e = listed(sp, i)
                    for j in range(12):
                        if j != 1:
                            sp.wait_ge(x_used, i * 12 + (j or 1))
                        if j < 8:
                            dst, src = xw[:, j % 2, :], w_gu[e, j * P:(j + 1) * P, :]
                        else:
                            dst = xw[:, j % 2, :].rearrange("p (k n) -> p k n", k=2)
                            src = w_down[e, (j - 8) * 2 * P:(j - 7) * 2 * P, :].rearrange("(k p) n -> p k n", p=P)
                        sp.dma_start(dst, src).then_inc(x_ready[j % 2], 16)
                extra_blocks(sp, body)

            @block.gpsimd
            def _(pool):
                def body(i):
                    pool.wait_ge(X.ids_read, i + 1)
                    pass_on(pool, X, i + 1)
                    pool_gather(pool, X)
                pool.wait_ge(M.marked, E + 1)
                nc.gpsimd.memset(mark[:], 0.0).then_inc(X.marked, 1)
                extra_blocks(pool, body)

            @block.scalar
            def _(act):
                def body(i):
                    act.wait_ge(X.xT_done, i * 2 + 2)
                    act_modulate(act, X)
                    act.wait_ge(X.gu_read, i * 2 + 2)
                    nc.scalar.activation(sig[:], gate[:], ACT.Sigmoid, scale=1.702).then_inc(X.sig_ready, 1)
                    act.wait_ge(X.y_done, i + 1)
                    for h in range(2):
                        nc.scalar.activation(ysb[:, h * BANK:(h + 1) * BANK], bank(Y0 + h), ACT.Copy) \
                            .then_inc(X.y_read, 1)
                    act.wait_ge(X.y_read, i * 2 + 2)
                    act.dma_start(row_blocks[i + E], ysb[:]).then_inc(X.y_stored, 16)
                    act.wait_ge(X.y_stored, i * 16 + 16)
                extra_blocks(act, body)

            @block.vector
            def _(dve):
                def body(i):
                    dve_onehot(dve, X, lambda t: posx[:, t, bass.ds(i, 1)])
                    dve.wait_ge(X.ids_done, i + 1)
                    dve_ids(dve, X)
                    e = listed(dve, i)
                    dve_sel(dve, X, ident3[:, bass.ds(e, 1)])
                    dve.wait_ge(X.up_done, i + 1)
                    nc.vector.tensor_scalar(gate[:].rearrange("p (b n) -> p b n", b=2), ps[:, 0:2, :], 7.0, None,
                                            ALU.min).then_inc(X.gu_read, 1)
                    nc.vector.tensor_scalar(up[:].rearrange("p (b n) -> p b n", b=2), ps[:, 2:4, :], 7.0, -7.0, ALU.min,
                                            ALU.max).then_inc(X.gu_read, 1)
                    dve.wait_ge(X.gu_read, i * 2 + 2)
                    nc.vector.scalar_tensor_tensor(out=up[:], in0=up[:], scalar=1.0, in1=gate[:], op0=ALU.add,
                                                   op1=ALU.mult).then_inc(X.ug_ready, 1)
                    dve.wait_ge(X.ug_ready, i + 1)
                    dve.wait_ge(X.sig_ready, i + 1)
                    nc.vector.tensor_tensor(up[:], up[:], sig[:], ALU.mult).then_inc(X.act_ready, 1)
                    for h in range(2):
                        dve.wait_ge(X.aT_done, i * 2 + 1 + h)
                        nc.vector.tensor_copy(aT[:, 4 * h:4 * h + 4, :].rearrange("p k n -> p (k n)"), bank(6 + h)) \
                            .then_inc(X.aT_read, 1)
                    dve.wait_ge(X.y_read, i * 2 + 2)
                extra_blocks(dve, body)

            @block.tensor
            def _(pe):
                def body(i):
                    def tile(j):
                        pe.wait_ge(x_ready[j % 2], i * 96 + 16 * (j // 2 + 1))
                        return xw[:, j % 2, :]

                    pe.wait_ge(X.onehot_ready, i + 1)
                    pe_ids(pe, X)
                    pe.wait_ge(X.gathered, i * 16 + 16)
                    pe_turn(pe, X.xT_done, xe)
                    pe.wait_ge(X.sel_ready, i + 1)
                    pe.wait_ge(X.xeT_read, i * 8 + 8)
                    for b in range(4):
                        nc.tensor.matmul(bank(b), sel[:], bparts[:, b * BANK:(b + 1) * BANK], start=True, stop=False)
                    for k in range(KD):
                        w = tile(k)
                        for b in range(4):
                            mm = nc.tensor.matmul(bank(b), xeT[:, k, :], w[:, b * BANK:(b + 1) * BANK], start=False,
                                                  stop=k == KD - 1)
                        mm.then_inc(x_used if k < KD - 1 else X.up_done, 1)
                    pe.wait_ge(X.act_ready, i + 1)
                    pe_turn(pe, X.aT_done, up, first=x_used)
                    pe.wait_ge(X.aT_read, i * 2 + 2)
                    pe.wait_ge(X.ids_read, i + 1)
                    for j in range(4):
                        w = tile(8 + j).rearrange("p (k n) -> p k n", k=2)
                        for kk in range(2):
                            k = 2 * j + kk
                            for h in range(2):
                                mm = nc.tensor.matmul(bank(Y0 + h), aT[:, k, :], w[:, kk, h * BANK:(h + 1) * BANK],
                                                      start=k == 0, stop=k == KD - 1)
                        if j < 3:
                            mm.then_inc(x_used, 1)
                    mm.then_inc(X.y_done, 1)
                    pe.wait_ge(X.y_read, i * 2 + 2)
                    nc.tensor.matmul(ps[:, 0, 0:P], ident, ident, start=True, stop=True).then_inc(x_used, 1)
                nc.tensor.matmul(ps[:, 0, 0:P], ident, ident, start=True, stop=True).then_inc(x_used, 1)
                extra_blocks(pe, body)
        moe_scope.close()

        late_scope = ctx.enter_context(ExitStack())
        hT = sbuf("hT_late", [P, KD, T], scope=late_scope)
        mT = sbuf("mT", [P, 2 * KD, T], scope=late_scope)
        rowstat = sbuf("rowstat", [P, 8, NT], scope=late_scope)

        def tokrows(ap):
            return ap.rearrange("(t p) n -> p t n", p=P)

        def norm_signals(tag):
            return Norm(*[sem(f"{tag}_{name}") for name in NORM_SIGNALS])

        def act_norm(act, N, t, src, junk, at, ready, value):
            act.wait_ge(ready, value)
            if t:
                act.wait_ge(N.sum, t)
            nc.scalar.activation(junk, src, ACT.Square, accum_out=rowstat[:, at, t:t + 1]).then_inc(N.sum, 1)
            act.wait_ge(N.mean, t + 1)
            nc.scalar.activation(rowstat[:, at + 1, t:t + 1], rowstat[:, at + 1, t:t + 1], ACT.Sqrt).then_inc(N.root, 1)

        def dve_norm(dve, N, t, at):
            dve.wait_ge(N.sum, t + 1)
            nc.vector.tensor_scalar(rowstat[:, at + 1, t:t + 1], rowstat[:, at, t:t + 1], 1.0 / D, EPS, ALU.mult,
                                    ALU.add).then_inc(N.mean, 1)
            dve.wait_ge(N.root, t + 1)
            nc.vector.reciprocal(rowstat[:, at + 1, t:t + 1], rowstat[:, at + 1, t:t + 1]).then_inc(N.inverse, 1)
            dve.wait_ge(N.inverse, t + 1)
            return rowstat[:, at + 1, t:t + 1]

        def pe_turn_rows(pe, src, jobs, ready, value):
            pe.wait_ge(ready, value)
            for k, j in enumerate(jobs):
                j.open(pe)
                for t in range(NT):
                    mm = nc.tensor.transpose(ps[:, j.bank, t * P:(t + 1) * P], src[:, t, k * P:(k + 1) * P], ident)
                    if k == 0 and t == 0:
                        stream.settle(mm)
                j.done(mm)

        def act_features(act, jobs, weight):
            for k, j in enumerate(jobs):
                j.filled(act)
                j.empty(nc.scalar.activation(hT[:, k, :], bank(j.bank), ACT.Copy, scale=vcol(weight, k)))

        scr = scratch
        xn = scr[:, 0:NT * D].rearrange("p (t n) -> p t n", t=NT)
        comb_scope = ctx.enter_context(ExitStack())
        GB = 4
        gbuf = scr[:, 4096:4096 + 4 * D].rearrange("p (b n) -> p b n", b=GB)
        acc = sbuf("acc", [P, 2, D], scope=comb_scope)
        bdown = sbuf("bdown", [E, D], scope=comb_scope)
        wT = sbuf("wT", [E, T], scope=comb_scope)
        w1b = sbuf("w1b", [P, D], scope=comb_scope)
        junk1 = sbuf("junk1", [P, D], scope=comb_scope)
        j_wt = psum.job(7, "dve")
        j_bd = {(t, h): psum.job(2 * (t % 3) + h, "dve") for t in range(NT) for h in range(2)}
        j_ev = [psum.job(k, "act") for k in range(KD)]
        comb_loads = signal("comb_loads")
        rowed = [signal(f"rowed{b}") for b in range(GB)]
        row_used = signal("row_used")
        acc_step = signal("acc_step")
        h_ready = signal("h_ready")
        x2_ready = signal("x2_ready")
        N1, N2 = norm_signals("norm_first"), norm_signals("norm_even")

        with nc.Block() as block:
            @block.sync
            def _(sp):
                comb_loads.on(sp.dma_start(bdown[:], A["b_down"][0]), 16)
                comb_loads.on(sp.dma_start(w1b[:], A["final_norm_w"].rearrange("(a n) -> a n", a=1)
                                           .to_broadcast([P, D])), 16)

            @block.gpsimd
            def _(pool):
                for n in range(NT * TOPK):
                    if n >= GB:
                        pool.wait_ge(row_used.sem, n - GB + 1)
                    rowed[n % GB].on(nc.gpsimd.indirect_dma_start(
                        gbuf[:, n % GB, :], None, y_dram, bass.IndirectOffsetOnAxis(ap=dest[:, n:n + 1], axis=0)), 16)

            def finish(dve, t):
                r = dve_norm(dve, N1, t, 0)
                x2_ready.on(nc.vector.scalar_tensor_tensor(out=res[:, t, :], in0=res[:, t, :], scalar=r, in1=w1b[:],
                                                           op0=ALU.mult, op1=ALU.mult))
                x2_ready.wait(dve)
                r = dve_norm(dve, N2, t, 2)
                nc.vector.tensor_scalar(xn[:, t, :], res[:, t, :], r, None, ALU.mult).then_inc(N2.scaled, 1)

            @block.vector
            def _(dve):
                j_wt.filled(dve)
                j_wt.empty(nc.vector.tensor_copy(wT[:], bank(7, T, E)))
                dve.wait_ge(comb_loads.sem, 32)
                for t in range(NT):
                    a = acc[:, t % 2, :]
                    for k in range(TOPK):
                        n = t * TOPK + k
                        dve.wait_ge(rowed[n % GB].sem, 16 * (n // GB + 1))
                        w = wk[:, t, k:k + 1]
                        if k == 0:
                            if t >= 2:
                                dve.wait_ge(h_ready.sem, t - 1)
                            for h in range(2):
                                cols = slice(h * BANK, (h + 1) * BANK)
                                j = j_bd[t, h]
                                j.filled(dve)
                                j.empty(nc.vector.scalar_tensor_tensor(
                                    out=a[:, cols], in0=gbuf[:, n % GB, cols], scalar=w, in1=bank(j.bank), op0=ALU.mult,
                                    op1=ALU.add))
                                j.emptied_for(dve)
                            row_used.on(nc.vector.memset(rowstat[:, 7, 0:1], 0.0))
                        else:
                            if k > 1:
                                row_used.wait(dve)
                            row_used.on(nc.vector.scalar_tensor_tensor(
                                out=a, in0=gbuf[:, n % GB, :], scalar=w, in1=a, op0=ALU.mult, op1=ALU.add))
                    row_used.wait(dve)
                    acc_step.on(nc.vector.tensor_tensor(a, a, g2b[:], ALU.mult))
                    acc_step.wait(dve)
                    h_ready.on(nc.vector.tensor_tensor(res[:, t, :], res[:, t, :], a, ALU.add))
                    if t:
                        finish(dve, t - 1)
                finish(dve, NT - 1)

            @block.scalar
            def _(act):
                for t in range(NT):
                    if t:
                        act.wait_ge(N2.sum, t)
                    act_norm(act, N1, t, res[:, t, :], junk1[:], 0, h_ready.sem, t + 1)
                    act.wait_ge(N1.sum, t + 1)
                    act_norm(act, N2, t, res[:, t, :], junk1[:], 2, x2_ready.sem, t + 1)
                act_features(act, j_ev, "even_norm_2")

            @block.tensor
            def _(pe):
                j_wt.open(pe)
                for t in range(NT):
                    mm = nc.tensor.transpose(ps[0:E, 7, t * P:(t + 1) * P], wtok[:, t, :], ident)
                    if t == 0:
                        stream.settle(mm)
                j_wt.done(mm)
                j_wt.emptied_for(pe)
                pe.wait_ge(comb_loads.sem, 32)
                for (t, h), j in j_bd.items():
                    j.open(pe)
                    j.done(nc.tensor.matmul(bank(j.bank), wT[:, t * P:(t + 1) * P], bdown[:, h * BANK:(h + 1) * BANK],
                                            start=True, stop=True))
                pe_turn_rows(pe, xn, j_ev, N2.scaled, NT)
        comb_scope.close()
        fT = scr[:, 0:KD * T].rearrange("p (k n) -> p k n", k=KD)
        zt = scr[:, 4096:8192].rearrange("p (t g n) -> p t g n", t=NT, g=2)
        j_fg = [psum.job(b, "act") for b in range(KD)]
        j_fi = [psum.job(b, "dve") for b in range(KD)]
        j_ch, j_sq = [], []
        for half in range(2):
            j_ch.append({(t, g): psum.job(2 * t + g, ("act", "dve")[g]) for t in range(NT) for g in range(2)})
            j_sq.append([psum.job(c, ("act", "dve")[c % 2]) for c in range(4)])
        j_fw = [psum.job(b, "dve") for b in range(KD)]

        with nc.Block() as block:
            @block.sync
            def _(sp):
                stream.load(sp, end_fourier, LATE_SLOTS)

            @block.scalar
            def _(act):
                for i, j in enumerate(j_fg):
                    j.filled(act)
                    j.empty(nc.scalar.activation(mT[:, i, :], bank(j.bank), ACT.Silu))
                for half in range(2):
                    for t in range(NT):
                        j = j_ch[half][t, 0]
                        j.filled(act)
                        j.empty(nc.scalar.activation(zt[:, t, 0, :], bank(j.bank), ACT.Copy))
                    for c in (0, 2):
                        j = j_sq[half][c]
                        j.filled(act)
                        j.empty(nc.scalar.activation(fT[:, 4 * half + c, :], bank(j.bank), ACT.Copy))

            @block.vector
            def _(dve):
                for i, j in enumerate(j_fi):
                    j.filled(dve)
                    j.empty(nc.vector.tensor_copy(fT[:, i, :], bank(j.bank)))
                for half in range(2):
                    for t in range(NT):
                        j = j_ch[half][t, 1]
                        j.filled(dve)
                        j.empty(nc.vector.tensor_copy(zt[:, t, 1, :], bank(j.bank)))
                    for c in (1, 3):
                        j = j_sq[half][c]
                        j.filled(dve)
                        j.empty(nc.vector.tensor_copy(fT[:, 4 * half + c, :], bank(j.bank)))
                for i, j in enumerate(j_fw):
                    j.filled(dve)
                    if i == 0:
                        j_fg[-1].emptied_for(dve)
                    j.empty(nc.vector.tensor_tensor(mT[:, i, :], mT[:, i, :], bank(j.bank), ALU.mult))

            @block.tensor
            def _(pe):
                def features(jobs):
                    return [(j, bank(j.bank), lambda k, w, kk, i=i: w[:, kk, i * P:(i + 1) * P],
                             lambda k, w, kk: hT[:, k, :]) for i, j in enumerate(jobs)]

                project(pe, 4, features(j_fg))
                project(pe, 4, features(j_fi))
                dc, sc, ss = take(pe), take(pe), take(pe)
                j_fi[-1].emptied_for(pe)
                for half in range(2):
                    for (t, g), j in j_ch[half].items():
                        j.open(pe)
                        for kk in range(2):
                            mm = nc.tensor.matmul(bank(j.bank), fT[:, 4 * half + 2 * g + kk, t * P:(t + 1) * P], dc[:, kk, :],
                                                  start=kk == 0, stop=kk == 1)
                        j.done(mm)
                    j_ch[half][NT - 1, 0].emptied_for(pe)
                    j_ch[half][NT - 1, 1].emptied_for(pe)
                    for c, j in enumerate(j_sq[half]):
                        j.open(pe)
                        for t in range(NT):
                            for part, table in enumerate((sc, ss)):
                                at = part * 256 + (c % 2) * P
                                mm = nc.tensor.matmul(bank(j.bank), zt[:, t, c // 2, at:at + P], table[:, t, :],
                                                      start=t == 0 and part == 0, stop=t == NT - 1 and part == 1)
                        j.done(mm)
                for _ in range(3):
                    stream.owe()
                fw = take(pe)
                for i, j in enumerate(j_fw):
                    g, e = i // 2, i % 2
                    if i in (0, 4):
                        for c in (2, 3):
                            j_sq[i // 4][c].emptied_for(pe)
                    j.open(pe)
                    for kk in range(2):
                        mm = nc.tensor.matmul(bank(j.bank), fw[:, 2 * g + kk, e * P:(e + 1) * P], fT[:, 2 * g + kk, :],
                                              start=kk == 0, stop=kk == 1)
                        if i == 0 and kk == 0:
                            stream.settle(mm)
                    j.done(mm)
                stream.owe()
        att_scope = ctx.enter_context(ExitStack())
        kv = sbuf("kv", [P, NT, 2, NKV * HD], scope=att_scope)
        kT2 = sbuf("kT2", [P, NKV, T], scope=att_scope)
        gtab = sbuf("gtab", [P, 4, NT, HD], scope=att_scope)
        prob = sbuf("prob", [P, NT, T], scope=att_scope)
        att = sbuf("att", [P, 4, NT], scope=att_scope)
        qs = scr[:, 0:4096].rearrange("p (t n) -> p t n", t=NT)
        tmpa, tmpb = scr[:, 4096:5120], scr[:, 5120:6144]
        rope = scr[:, 6144:7168].rearrange("p (s t n) -> p s t n", s=2, t=NT)
        gains = scr[:, 7168:7424].rearrange("p (s n) -> p s n", s=2)
        qss = rowstat[:].rearrange("p a t -> p (a t)")[:, 0:8]
        probT = scr[:, 4096:8192].rearrange("p (b k n) -> p b k n", b=2, k=NT)
        j_kv = [psum.job(t, "act") for t in range(NT)]
        j_q = {(t, h): psum.job(4 + h if t == 0 else (6 + h if t == 1 else 2 * (t - 2) + h), "act")
               for t in range(NT) for h in range(2)}
        j_ag = [psum.job((4 + b) % 8, "act") for b in range(KD)]
        j_kt = [psum.job(4 + h, "act") for h in range(NKV)]
        j_qt = [psum.job((6 + h) % 8, ("act", "dve")[h % 2]) for h in range(NQ)]
        j_sc, j_pt, j_pv = {}, {}, {}
        for step_ in range(NQ + 2):
            for t in range(NT):
                if 1 <= step_ <= NQ:
                    j_pt[step_ - 1, t] = psum.job(4 + t % 2, "act")
                if step_ < NQ:
                    j_sc[step_, t] = psum.job(t, "act")
            if step_ >= 2:
                j_pv[step_ - 2] = psum.job(6 + step_ % 2, "dve")
        rope_loads = signal("rope_loads")
        gtab_step = signal("gtab_step")
        rn = signal("rn")
        rn_root = signal("rn_root")
        rot = signal("rot")
        mx = signal("mx")
        nmx = signal("nmx")
        inv = signal("inv")
        normed = signal("normed")
        rotated = {}
        groups = [("k", t) for t in range(NT)] + [("q", t) for t in range(NT)]

        def head_rows(kind, t):
            return (kv[:, t, 0, :], NKV) if kind == "k" else (qs[:, t, :], NQ)

        with nc.Block() as block:
            @block.sync
            def _(sp):
                rope_loads.on(sp.dma_start(rope[:, 0], tokrows(A["rope"][0])), 16)
                rope_loads.on(sp.dma_start(rope[:, 1], tokrows(A["rope"][1])), 16)
                rope_loads.on(sp.dma_start(gains[:, 0, :], A["q_gain_2"][0:1, :].to_broadcast([P, HD])), 16)
                rope_loads.on(sp.dma_start(gains[:, 1, :], A["k_gain_2"][0:1, :].to_broadcast([P, HD])), 16)
                stream.load(sp, end_qkv, LATE_SLOTS)

            def turn_out(act, h, t):
                if h >= 2 and t == 0:
                    j_pv[h - 2].filled(act)
                j_pt[h, t].empty(nc.scalar.activation(
                    probT[:, h % 2, :, t * P:(t + 1) * P], bank(j_pt[h, t].bank).rearrange("p (k n) -> p k n", k=NT),
                    ACT.Copy))

            @block.scalar
            def _(act):
                for t, j in enumerate(j_kv):
                    j.filled(act)
                    j.empty(nc.scalar.activation(kv[:, t, :, :].rearrange("p s n -> p (s n)"), bank(j.bank), ACT.Copy))
                for (t, h), j in j_q.items():
                    j.filled(act)
                    j.empty(nc.scalar.activation(qs[:, t, h * BANK:(h + 1) * BANK], bank(j.bank), ACT.Copy))
                for n in range(len(groups)):
                    act.wait_ge(rn.sem, 2 * n + 1)
                    rn_root.on(nc.scalar.activation(qss, qss, ACT.Sqrt))
                for i, j in enumerate(j_ag):
                    j.filled(act)
                    j.empty(nc.scalar.activation(mT[:, KD + i, :], bank(j.bank), ACT.Silu))
                for h, j in enumerate(j_kt):
                    j.filled(act)
                    j.empty(nc.scalar.activation(kT2[:, h, :], bank(j.bank), ACT.Copy))
                for h, j in enumerate(j_qt):
                    if h % 2 == 0:
                        j.filled(act)
                        j.empty(nc.scalar.activation(hT[:, h, :], bank(j.bank), ACT.Copy))
                for step_ in range(NQ + 1):
                    if step_ < NQ:
                        for t in range(NT):
                            j = j_sc[step_, t]
                            if step_ > 0:
                                j_pt[step_ - 1, t].filled(act)
                                turn_out(act, step_ - 1, t)
                            act.wait_ge(nmx.sem, 4 * step_ + t + 1)
                            j.empty(nc.scalar.activation(prob[:, t, :], bank(j.bank), ACT.Exp, scale=HD ** -0.5,
                                                         bias=att[:, 1, t:t + 1], accum_out=att[:, 2, t:t + 1]))
                    else:
                        for t in range(NT):
                            j_pt[step_ - 1, t].filled(act)
                            turn_out(act, step_ - 1, t)

            @block.vector
            def _(dve):
                dve.wait_ge(rope_loads.sem, 64)
                for s in range(2):
                    g = gains[:, s, :]
                    gtab_step.on(nc.vector.tensor_tensor(gtab[:, 2 * s], rope[:, 0],
                                                         g.unsqueeze(1).to_broadcast([P, NT, HD]), ALU.mult))
                    for b in range(4):
                        to, of = slice(32 * b, 32 * b + 32), slice(32 * (b ^ 1), 32 * (b ^ 1) + 32)
                        gtab_step.on(nc.vector.tensor_tensor(
                            gtab[:, 2 * s + 1, :, to], rope[:, 1, :, to],
                            g[:, of].unsqueeze(1).to_broadcast([P, NT, 32]), ALU.mult))
                gtab_step.wait(dve)
                for n, (kind, t) in enumerate(groups):
                    rows, heads = head_rows(kind, t)
                    if kind == "k":
                        j_kv[t].emptied_for(dve)
                    else:
                        j_q[t, 1].emptied_for(dve)
                    ta, tb = tmpa[:, 0:heads * HD], tmpb[:, 0:heads * HD]
                    by_head = lambda ap: ap.rearrange("p (h n) -> p h n", n=HD)
                    if n:
                        rot.wait(dve)
                    rot.on(nc.vector.tensor_tensor(ta, rows, rows, ALU.mult))
                    rot.wait(dve)
                    rot.on(nc.vector.tensor_reduce(qss[:, 0:heads], by_head(ta), AX.X, ALU.add))
                    rot.wait(dve)
                    if n == 0:
                        rot.on(nc.vector.memset(qss[:, heads:8], 1.0))
                        rot.wait(dve)
                    rn.on(nc.vector.tensor_scalar(qss[:, 0:heads], qss[:, 0:heads], 1.0 / HD, EPS, ALU.mult, ALU.add))
                    dve.wait_ge(rn_root.sem, n + 1)
                    rn.on(nc.vector.reciprocal(qss[:, 0:heads], qss[:, 0:heads]))
                    rn.wait(dve)
                    rot.on(nc.vector.tensor_tensor(by_head(rows), by_head(rows),
                                                   qss[:, 0:heads].unsqueeze(2).to_broadcast([P, heads, HD]), ALU.mult))
                    rot.wait(dve)
                    s = 0 if kind == "q" else 2
                    rot.on(nc.vector.tensor_tensor(by_head(ta), by_head(rows),
                                                   gtab[:, s, t:t + 1, :].to_broadcast([P, heads, HD]), ALU.mult))
                    for b in range(2):
                        half = lambda ap, q: ap.rearrange("p (h a s n) -> p h a s n", a=2, s=2, n=32)[:, :, :, q, :]
                        sine = gtab[:, s + 1, t, :].rearrange("p (a s n) -> p a s n", a=2, s=2)[:, :, b, :]
                        rot.on(nc.vector.tensor_tensor(half(tb, b), half(rows, 1 - b),
                                                       sine.unsqueeze(1).to_broadcast([P, heads, 2, 32]), ALU.mult))
                    rot.wait(dve)
                    rot.on(nc.vector.tensor_tensor(rows, ta, tb, ALU.add))
                    rotated[kind, t] = rot.n
                for h, j in enumerate(j_qt):
                    if h % 2:
                        j.filled(dve)
                        j.empty(nc.vector.tensor_copy(hT[:, h, :], bank(j.bank)))

                def normalise(h, t):
                    j_sc[h, t].emptied_for(dve)
                    inv.on(nc.vector.reciprocal(att[:, 3, t:t + 1], att[:, 2, t:t + 1]))
                    inv.wait(dve)
                    normed.on(nc.vector.tensor_scalar(prob[:, t, :], prob[:, t, :], att[:, 3, t:t + 1], None, ALU.mult))

                for step_ in range(NQ + 2):
                    for t in range(NT):
                        if step_ < NQ:
                            j_sc[step_, t].filled(dve)
                            if step_:
                                j_sc[step_ - 1, t].emptied_for(dve)
                            mx.on(nc.vector.tensor_reduce(att[:, 0, t:t + 1], bank(j_sc[step_, t].bank), AX.X, ALU.max))
                            mx.wait(dve)
                            nmx.on(nc.vector.tensor_scalar(att[:, 1, t:t + 1], att[:, 0, t:t + 1], -(HD ** -0.5), None,
                                                           ALU.mult))
                        if step_ < NQ and t:
                            normalise(step_, t - 1)
                    if step_ < NQ:
                        normalise(step_, NT - 1)
                    if step_ >= 2:
                        h = step_ - 2
                        j_pv[h].filled(dve)
                        if h == 0:
                            j_ag[-1].emptied_for(dve)
                        j_pv[h].empty(nc.vector.tensor_tensor(mT[:, KD + h, :], mT[:, KD + h, :], bank(j_pv[h].bank),
                                                              ALU.mult))

            @block.tensor
            def _(pe):
                project(pe, 2, [(j, bank(j.bank), lambda k, w, kk, t=t: hT[:, k, t * P:(t + 1) * P],
                                 lambda k, w, kk: w[:, kk, :]) for t, j in enumerate(j_kv)])
                project(pe, 4, [(j, bank(j.bank), lambda k, w, kk, t=t: hT[:, k, t * P:(t + 1) * P],
                                 lambda k, w, kk, h=h: w[:, kk, h * BANK:(h + 1) * BANK]) for (t, h), j in j_q.items()])
                project(pe, 4, [(j, bank(j.bank), lambda k, w, kk, i=i: w[:, kk, i * P:(i + 1) * P],
                                 lambda k, w, kk: hT[:, k, :]) for i, j in enumerate(j_ag)])
                pe.wait_ge(rot.sem, rotated["k", NT - 1])
                for h, j in enumerate(j_kt):
                    j.open(pe)
                    for t in range(NT):
                        mm = nc.tensor.transpose(ps[:, j.bank, t * P:(t + 1) * P], kv[:, t, 0, h * HD:(h + 1) * HD], ident)
                        if h == 0 and t == 0:
                            stream.settle(mm)
                    j.done(mm)
                pe.wait_ge(rot.sem, rotated["q", NT - 1])
                for h, j in enumerate(j_qt):
                    j.open(pe)
                    for t in range(NT):
                        mm = nc.tensor.transpose(ps[:, j.bank, t * P:(t + 1) * P], qs[:, t, h * HD:(h + 1) * HD], ident)
                    j.done(mm)
                j_qt[-2].emptied_for(pe)
                j_qt[-1].emptied_for(pe)
                for step_ in range(NQ + 2):
                    for t in range(NT):
                        if 1 <= step_ <= NQ:
                            h = step_ - 1
                            j = j_pt[h, t]
                            pe.wait_ge(normed.sem, 4 * h + t + 1)
                            j.open(pe)
                            for k in range(NT):
                                mm = nc.tensor.transpose(ps[:, j.bank, k * P:(k + 1) * P], prob[:, t, k * P:(k + 1) * P],
                                                         ident)
                            j.done(mm)
                        if step_ < NQ:
                            h = step_
                            j = j_sc[h, t]
                            j.open(pe)
                            j.done(nc.tensor.matmul(bank(j.bank), hT[:, h, t * P:(t + 1) * P],
                                                    kT2[:, h * NKV // NQ, :], start=True, stop=True))
                    if step_ >= 2:
                        h = step_ - 2
                        j = j_pv[h]
                        j.open(pe)
                        j_pt[h, NT - 1].emptied_for(pe)
                        g = h * NKV // NQ
                        for k in range(NT):
                            mm = nc.tensor.matmul(bank(j.bank), kv[:, k, 1, g * HD:(g + 1) * HD], probT[:, h % 2, k, :],
                                                  start=k == 0, stop=k == NT - 1)
                        j.done(mm)
        att_scope.close()
        junk2 = scr[:, 4096:4096 + D]
        j_eo = {(t, h): psum.job(4 * h + t, "dve") for h in range(2) for t in range(NT)}
        j_on = [psum.job(k, "act") for k in range(KD)]
        N3 = norm_signals("norm_odd")
        with nc.Block() as block:
            @block.sync
            def _(sp):
                stream.load(sp, end_even, LATE_SLOTS)

            @block.scalar
            def _(act):
                for t in range(NT):
                    act_norm(act, N3, t, res[:, t, :], junk2, 0, psum.free["dve"], j_eo[t, 1].emptied)
                act_features(act, j_on, "odd_norm_2")

            @block.vector
            def _(dve):
                for (t, h), j in j_eo.items():
                    cols = slice(h * BANK, (h + 1) * BANK)
                    j.filled(dve)
                    j.empty(nc.vector.tensor_tensor(res[:, t, cols], res[:, t, cols], bank(j.bank), ALU.add))
                for t in range(NT):
                    r = dve_norm(dve, N3, t, 0)
                    nc.vector.tensor_scalar(xn[:, t, :], res[:, t, :], r, None, ALU.mult).then_inc(N3.scaled, 1)

            @block.tensor
            def _(pe):
                project(pe, 8, [(j, bank(j.bank), lambda k, w, kk, t=t: mT[:, k, t * P:(t + 1) * P],
                                 lambda k, w, kk, h=h: w[:, kk, h * BANK:(h + 1) * BANK]) for (t, h), j in j_eo.items()])
                pe_turn_rows(pe, xn, j_on, N3.scaled, NT)
        NB = 4
        rnn_scope = ctx.enter_context(ExitStack())
        xr = sbuf("xr", [P, NB, T + 3], scope=rnn_scope)
        hf = sbuf("hf", [P, NB, T], scope=rnn_scope)
        tmp = sbuf("rnn_tmp", [P, NB, T], scope=rnn_scope)
        decay_c = sbuf("decay_c", [P, 4, 2 * NR], scope=rnn_scope)
        blk = lambda i: scr[:, i * NB * T:(i + 1) * NB * T].rearrange("p (b n) -> p b n", b=NB)
        xcv, ig, rg, ag = (blk(i) for i in range(4))
        lam = vcol("rglru_lambda_2", 0, 2 * NR)
        j_in, j_gt = [], []
        for p in range(4):
            j_in.append([psum.job(b, "act") for b in range(2 * NB)])
            j_gt.append({(d, g, b): psum.job(4 * g + b, "act") for d in range(2) for g in range(2) for b in range(NB)})
        pads = signal("pads")
        dc_step = signal("dc_step")
        dc_act = signal("dc_act")
        conv = signal("conv")
        expo = signal("expo")
        rec = signal("rec")
        rooted = signal("rooted")
        j_oo = {(t, h): psum.job(2 * t + h, "dve") for t in range(NT) for h in range(2)}
        wfb = sbuf("wfb", [P, D], scope=rnn_scope)
        junk4 = sbuf("junk4", [P, D], scope=rnn_scope)
        last_load = signal("last_load")
        N4 = norm_signals("norm_last")

        with nc.Block() as block:
            @block.sync
            def _(sp):
                last_load.on(sp.dma_start(wfb[:], A["final_norm_2"].rearrange("(a n) -> a n", a=1).to_broadcast([P, D])),
                             16)
                stream.load(sp, len(stream.tiles) + 2, LATE_SLOTS)
                for t in range(NT):
                    sp.wait_ge(N4.scaled, t + 1)
                    stored.on(sp.dma_start(out[0, t * P:(t + 1) * P, :], res[:, t, :]), 16)
                stored.wait(sp)

            @block.gpsimd
            def _(pool):
                pads.on(nc.gpsimd.memset(xr[:, :, 0:2], 0.0))
                pads.on(nc.gpsimd.memset(xr[:, :, T + 2:T + 3], 0.0))

            def rec_at(p, d, k):
                return 18 * p + 8 * d + k

            @block.vector
            def _(dve):
                def step(ins):
                    dc_step.on(ins)
                    dc_step.wait(dve)

                e, s, s2, q = (decay_c[:, i, :] for i in range(4))
                dve.wait_ge(dc_act.sem, 2)
                step(nc.vector.tensor_scalar(s, e, 2.0, None, ALU.add))
                step(nc.vector.reciprocal(s, s))
                step(nc.vector.tensor_tensor(s, s, e, ALU.mult))
                step(nc.vector.tensor_tensor(s2, s, s, ALU.mult))
                step(nc.vector.tensor_scalar(q, s2, 1.0 / 17, None, ALU.mult))
                for n in (15, 13, 11, 9, 7, 5, 3):
                    step(nc.vector.scalar_tensor_tensor(out=q, in0=q, scalar=1.0 / n, in1=s2, op0=ALU.add, op1=ALU.mult))
                step(nc.vector.scalar_tensor_tensor(out=s, in0=q, scalar=1.0, in1=s, op0=ALU.add, op1=ALU.mult))
                step(nc.vector.tensor_scalar(q, lam, -1.0, 0.0, ALU.mult, ALU.max))
                step(nc.vector.scalar_tensor_tensor(out=s, in0=s, scalar=2.0, in1=q, op0=ALU.mult, op1=ALU.add))
                step(nc.vector.tensor_scalar(decay_c[:, 0, :], s, -8.0, None, ALU.mult))
                step(nc.vector.tensor_scalar(decay_c[:, 1, :], s, 8.0, None, ALU.mult))
                dve.wait_ge(pads.sem, 2)
                for p in range(4):
                    for b in range(NB):
                        i = NB * p + b
                        j_in[p][b].emptied_for(dve)
                        cw = lambda j: vcol("conv_w_2", j * NR + i)
                        conv.on(nc.vector.tensor_scalar(xcv[:, b, :], xr[:, b, 0:T], cw(0), vcol("conv_b_2", i),
                                                        ALU.mult, ALU.add))
                        for j in range(1, 4):
                            conv.wait(dve)
                            conv.on(nc.vector.scalar_tensor_tensor(out=xcv[:, b, :], in0=xr[:, b, j:j + T], scalar=cw(j),
                                                                   in1=xcv[:, b, :], op0=ALU.mult, op1=ALU.add))
                    conv.wait(dve)
                    for d in range(2):
                        n = 2 * p + d
                        h = hf if d == 0 else tmp
                        dve.wait_ge(expo.sem, 8 * n + 8)
                        rec.on(nc.vector.tensor_tensor(tmp[:], ag, ag, ALU.mult))
                        rec.wait(dve)
                        rec.on(nc.vector.scalar_tensor_tensor(out=rg, in0=tmp[:], scalar=1.0, in1=rg, op0=ALU.add,
                                                              op1=ALU.mult))
                        rec.on(nc.vector.tensor_tensor(ig, ig, xcv, ALU.mult))
                        rec.wait(dve)
                        dve.wait_ge(rooted.sem, n + 1)
                        rec.on(nc.vector.tensor_tensor(rg, rg, ig, ALU.mult))
                        rec.wait(dve)
                        way = 1 if d == 0 else -1
                        for b in range(NB):
                            rec.on(nc.vector.tensor_tensor_scan(h[:, b, ::way], ag[:, b, ::way], rg[:, b, ::way], 0.0,
                                                                ALU.mult, ALU.add))
                        rec.wait(dve)
                    rec.on(nc.vector.tensor_tensor(hf[:], hf[:], tmp[:], ALU.add))
                    rec.wait(dve)
                    rec.on(nc.vector.tensor_tensor(mT[:, NB * p:NB * p + NB, :], mT[:, NB * p:NB * p + NB, :], hf[:],
                                                   ALU.mult))
                    rec.wait(dve)

                def finish(t):
                    r = dve_norm(dve, N4, t, 0)
                    nc.vector.scalar_tensor_tensor(out=res[:, t, :], in0=res[:, t, :], scalar=r, in1=wfb[:], op0=ALU.mult,
                                                   op1=ALU.mult).then_inc(N4.scaled, 1)

                dve.wait_ge(last_load.sem, 16)
                for (t, h), j in j_oo.items():
                    cols = slice(h * BANK, (h + 1) * BANK)
                    j.filled(dve)
                    j.empty(nc.vector.tensor_tensor(res[:, t, cols], res[:, t, cols], bank(j.bank), ALU.add))
                    if h and t:
                        finish(t - 1)
                finish(NT - 1)

            @block.scalar
            def _(act):
                dc_act.on(nc.scalar.activation(decay_c[:, 0, :], lam, ACT.Abs))
                dc_act.wait(act)
                dc_act.on(nc.scalar.activation(decay_c[:, 0, :], decay_c[:, 0, :], ACT.Exp, scale=-1.0))

                def inputs(p):
                    for b, j in enumerate(j_in[p]):
                        j.filled(act)
                        if b < NB:
                            if p:
                                act.wait_ge(conv.sem, 16 * p)
                            j.empty(nc.scalar.activation(xr[:, b, 2:2 + T], bank(j.bank), ACT.Copy))
                        else:
                            j.empty(nc.scalar.activation(mT[:, NB * p + b - NB, :], bank(j.bank), ACT.Silu))

                def gates(p, d):
                    if p or d:
                        act.wait_ge(rec.sem, rec_at(p, d, 0) - (2 if d == 0 else 0))
                    for g in range(2):
                        for b in range(NB):
                            j = j_gt[p][d, g, b]
                            i = NB * p + b
                            j.filled(act)
                            j.empty(nc.scalar.activation((rg, ig)[g][:, b, :], bank(j.bank), ACT.Sigmoid,
                                                         bias=vcol(("gate_a_b_2", "gate_x_b_2")[g], d * NR + i)))
                    j_gt[p][d, 1, NB - 1].emptied_for(act)
                    for b in range(NB):
                        i = NB * p + b
                        expo.on(nc.scalar.activation(ag[:, b, :], rg[:, b, :], ACT.Exp,
                                                     scale=decay_c[:, 0, d * NR + i:d * NR + i + 1]))
                    expo.wait(act)
                    for b in range(NB):
                        i = NB * p + b
                        expo.on(nc.scalar.activation(rg[:, b, :], rg[:, b, :], ACT.Tanh,
                                                     scale=decay_c[:, 1, d * NR + i:d * NR + i + 1]))
                    act.wait_ge(rec.sem, rec_at(p, d, 2))
                    rooted.on(nc.scalar.activation(rg, rg, ACT.Sqrt))

                inputs(0)
                act.wait_ge(dc_step.sem, 17)
                for p in range(4):
                    gates(p, 0)
                    gates(p, 1)
                    if p < 3:
                        inputs(p + 1)
                for t in range(NT):
                    act_norm(act, N4, t, res[:, t, :], junk4[:], 0, psum.free["dve"], j_oo[t, 1].emptied)

            @block.tensor
            def _(pe):
                def inputs(p):
                    project(pe, 4, [(j, bank(j.bank), lambda k, w, kk, b=b: w[:, kk, b * P:(b + 1) * P],
                                     lambda k, w, kk: hT[:, k, :]) for b, j in enumerate(j_in[p])])

                for p in range(4):
                    inputs(p)
                    w = take(pe)
                    pe.wait_ge(conv.sem, 16 * (p + 1))
                    for n, ((d, g, b), j) in enumerate(j_gt[p].items()):
                        j.open(pe)
                        mm = nc.tensor.matmul(bank(j.bank), w[:, (2 * d + g) * NB + b, :], xcv[:, b, :], start=True,
                                              stop=True)
                        j.done(mm)
                    stream.owe()
                pe.wait_ge(rec.sem, rec_at(3, 0, 0))
                project(pe, 8, [(j, bank(j.bank), lambda k, w, kk, t=t: mT[:, k, t * P:(t + 1) * P],
                                 lambda k, w, kk, h=h: w[:, kk, h * BANK:(h + 1) * BANK]) for (t, h), j in j_oo.items()],
                        before={3 * NB: lambda: pe.wait_ge(rec.sem, rec_at(4, 0, 0))})
        rnn_scope.close()


def constants():
    import numpy as np
    cst = np.zeros((P, C_N), np.float32)
    p, j = np.arange(P)[:, None], np.arange(P)[None, :]
    cst[:, C_ID:C_ID + P] = p == j
    same = p // CHUNK == j // CHUNK
    cst[:, C_MF:C_MF + P] = same & (p <= j)
    cst[:, C_MB:C_MB + P] = same & (p >= j)
    cst[:, C_IOTA1:C_IOTA1 + P] = j + 1
    cst[:, C_TRI:C_TRI + P] = p < j
    cst[:, C_ONES:C_ONES + P] = 1
    cst[:, C_IOTA32:C_IOTA32 + E] = np.arange(E)
    cst[:, C_TOK:C_TOK + NT] = p + P * np.arange(NT)
    cst[:, C_RESET:C_RESET + T + TC] = np.arange(T + TC) % CHUNK != 0
    cst[:, C_XI:C_XI + XB] = np.arange(XB)
    cst[:, C_ID3:C_ID3 + E] = p % E == np.arange(E)
    rows, width = T // 64, 64
    r, c = np.arange(T) // width, np.arange(T) % width
    pool = np.zeros((4, T, T), np.float64)
    for g, w in enumerate((2, 4, 8, 16)):
        lo, hi = w // 2, w - 1 - w // 2
        near = ((r[:, None] >= r[None, :] - lo) & (r[:, None] <= r[None, :] + hi)
                & (c[:, None] >= c[None, :] - lo) & (c[:, None] <= c[None, :] + hi))
        pool[g] = near / near.sum(0, keepdims=True) - np.eye(T)
    n = np.arange(256)
    ang = 2 * np.pi * (np.outer(n, n) % 256) / 256
    dft_c = np.concatenate([np.cos(ang), np.sin(ang)], 1) / 16
    n = np.arange(T)
    ang = 2 * np.pi * (np.outer(n, n) % T) / T
    dft_s = np.stack([np.cos(ang), -np.sin(ang)]) / np.sqrt(T)
    inv = (np.float32(10000.0) ** (-np.arange(0, 64, 2, dtype=np.float32) / np.float32(64))).astype(np.float32)
    ar = (r.astype(np.float32)[:, None] * inv).astype(np.float64)
    ac = (c.astype(np.float32)[:, None] * inv).astype(np.float64)
    rope = np.stack([np.concatenate([np.cos(ar), np.cos(ar), np.cos(ac), np.cos(ac)], 1),
                     np.concatenate([-np.sin(ar), np.sin(ar), -np.sin(ac), np.sin(ac)], 1)])
    f = lambda a: np.ascontiguousarray(a, np.float32)
    return {"cst": cst, "pool_mat": f(pool), "dft_c": f(dft_c), "dft_s": f(dft_s), "rope": f(rope)}


WHOLE = ["x", "ctx", "w_ada", "w_in", "w_gk_f", "w_gk_b", "w_pool", "w_out", "w_router", "b_router", "w_gu", "b_gu",
         "w_down", "b_down", "final_norm_w", "even_w_in_2", "fourier_w_2", "q_gain_2", "k_gain_2", "even_w_out_2",
         "odd_w_in_2", "gate_a_w_2", "gate_x_w_2", "odd_w_out_2", "final_norm_2"]


def kernel(**inputs):
    import numpy as np
    import concourse.bacc as bacc
    from concourse.bass_utils import run_bass_kernel_spmd

    nc = bacc.Bacc("TRN2", target_bir_lowering=False, num_devices=1)
    arrays = {name: np.ascontiguousarray(inputs[name]) for name in WHOLE}
    for name, n in VECS:
        arrays[name] = np.ascontiguousarray(inputs[name]).reshape(n, P)
    arrays["b_ada_row"] = np.ascontiguousarray(inputs["b_ada"])
    arrays.update(constants())
    A = {name: nc.dram_tensor(f"in_{name}", a.shape, mybir.dt.from_np(a.dtype), kind="ExternalInput").ap()
         for name, a in arrays.items()}
    out = nc.dram_tensor("out_0", (1, T, D), F32, kind="ExternalOutput").ap()
    build(nc, A, out)
    launched = run_bass_kernel_spmd(nc, [{f"in_{name}": a for name, a in arrays.items()}], core_ids=[0])
    return launched.results[0]["out_0"]
```
